# Optimizing a Trainium2 kernel written in Bass

```python
import jax, jax.numpy as jnp
from jax import lax
import numpy as np

D_MODEL = 2048
BATCH = 1
SEQ = 256
DEPTH = 1

CHUNK = 64
Q_BLOCK = 128
MIX_WIDTH = D_MODEL
EPS = 1e-6
MLA_HEADS = 8
MLA_Q_LORA = 512
MLA_KV_LORA = 256
MLA_NOPE = 128
MLA_ROPE = 64
MLA_V = 128
ROPE_BASE = 10000.0
SB_HEADS = 8
SB_DIM = 64
FOX_HEADS = 8
FOX_DIM = 64
IN_SIZES = (MLA_Q_LORA, MLA_KV_LORA, MLA_ROPE, 3 * SB_HEADS * SB_DIM, 3 * FOX_HEADS * FOX_DIM, FOX_HEADS)
IN_WIDTH = MLA_Q_LORA + MLA_KV_LORA + MLA_ROPE + 3 * SB_HEADS * SB_DIM + 3 * FOX_HEADS * FOX_DIM + FOX_HEADS
OUT_SIZES = (MLA_HEADS * MLA_V, SB_HEADS * SB_DIM, FOX_HEADS * FOX_DIM)
D_FF = 4 * D_MODEL

kernel_name = 'hybrid_mla_stickbreak_fox_block'

def rms_norm(x, g):
    xf = x.astype(jnp.float32)
    y = xf * lax.rsqrt(jnp.mean(xf * xf, axis=-1, keepdims=True) + EPS)
    return (y * g.astype(jnp.float32)).astype(x.dtype)

def split_sizes(p, sizes):
    idx, acc = [], 0
    for s in sizes[:-1]:
        acc += s
        idx.append(acc)
    return jnp.split(p, idx, axis=-1)

def rope_tables(seq_len, dim):
    pos = jnp.arange(seq_len, dtype=jnp.float32)
    inv = ROPE_BASE ** (-jnp.arange(0, dim, 2, dtype=jnp.float32) / dim)
    ang = pos[:, None] * inv[None, :]
    return jnp.cos(ang), jnp.sin(ang)

def apply_rope(x, cos, sin):
    x1, x2 = jnp.split(x.astype(jnp.float32), 2, axis=-1)
    return jnp.concatenate([x1 * cos - x2 * sin, x2 * cos + x1 * sin], axis=-1).astype(x.dtype)

def head_rms_norm(o, g):
    B, S, H, d = o.shape
    return rms_norm(o, g.reshape(H, d)).reshape(B, S, H * d)

def mla_attention(q_nope, q_rope, k_nope, k_rope, v):
    S = q_nope.shape[1]
    scale = (MLA_NOPE + MLA_ROPE) ** -0.5
    outs = []
    for i in range(S // Q_BLOCK):
        q0, q1 = i * Q_BLOCK, (i + 1) * Q_BLOCK
        s = (jnp.einsum('bqhd,bkhd->bhqk', q_nope[:, q0:q1], k_nope[:, :q1])
             + jnp.einsum('bqhd,bkd->bhqk', q_rope[:, q0:q1], k_rope[:, :q1])).astype(jnp.float32) * scale
        t_pos = jnp.arange(q0, q1)[:, None]
        s_pos = jnp.arange(q1)[None, :]
        allowed = s_pos < (t_pos // CHUNK + 1) * CHUNK
        p = jax.nn.softmax(jnp.where(allowed, s, -jnp.inf), axis=-1)
        outs.append(jnp.einsum('bhqk,bkhd->bqhd', p.astype(v.dtype), v[:, :q1]))
    return jnp.concatenate(outs, axis=1)

def stick_breaking_attention(q, k, v):
    S, d = q.shape[1], q.shape[3]
    scale = d ** -0.5
    outs = []
    for i in range(S // Q_BLOCK):
        q0, q1 = i * Q_BLOCK, (i + 1) * Q_BLOCK
        z = jnp.einsum('bqhd,bkhd->bhqk', q[:, q0:q1], k[:, :q1]).astype(jnp.float32) * scale
        t_pos = jnp.arange(q0, q1)[:, None]
        s_pos = jnp.arange(q1)[None, :]
        strict = s_pos < t_pos
        log_keep = jnp.where(strict, jax.nn.log_sigmoid(-z), 0.0)
        log_stick = lax.cumsum(log_keep, axis=3, reverse=True) - log_keep
        a = jnp.where(strict, jnp.exp(jax.nn.log_sigmoid(z) + log_stick), 0.0)
        outs.append(jnp.einsum('bhqk,bkhd->bqhd', a.astype(v.dtype), v[:, :q1]))
    return jnp.concatenate(outs, axis=1)

def forgetting_attention(q, k, v, log_f):
    S, d = q.shape[1], q.shape[3]
    scale = d ** -0.5
    F = jnp.swapaxes(jnp.cumsum(log_f, axis=1), 1, 2)
    outs = []
    for i in range(S // Q_BLOCK):
        q0, q1 = i * Q_BLOCK, (i + 1) * Q_BLOCK
        s = jnp.einsum('bqhd,bkhd->bhqk', q[:, q0:q1], k[:, :q1]).astype(jnp.float32) * scale
        s = s + F[:, :, q0:q1, None] - F[:, :, None, :q1]
        t_pos = jnp.arange(q0, q1)[:, None]
        s_pos = jnp.arange(q1)[None, :]
        p = jax.nn.softmax(jnp.where(s_pos <= t_pos, s, -jnp.inf), axis=-1)
        outs.append(jnp.einsum('bhqk,bkhd->bqhd', p.astype(v.dtype), v[:, :q1]))
    return jnp.concatenate(outs, axis=1)

def setup_inputs(seed: int = 0) -> dict:
    key = jax.random.key(seed)
    ks = jax.random.split(key, 20)
    n = jax.random.normal
    f32 = jnp.float32
    L, D = DEPTH, D_MODEL
    return {
        'x': n(ks[0], (BATCH, SEQ, D), f32),
        'c': n(ks[1], (BATCH, D), f32),
        'w_ada': n(ks[2], (L, D, 6 * D), f32) * (0.5 * D ** -0.5),
        'b_ada': n(ks[3], (L, 6 * D), f32) * 0.01,
        'norm_mix': 1.0 + 0.02 * n(ks[4], (L, D), f32),
        'w_in': n(ks[5], (L, D, IN_WIDTH), f32) * D ** -0.5,
        'q_norm': 1.0 + 0.02 * n(ks[6], (L, MLA_Q_LORA), f32),
        'w_uq': n(ks[7], (L, MLA_Q_LORA, MLA_HEADS * (MLA_NOPE + MLA_ROPE)), f32) * MLA_Q_LORA ** -0.5,
        'kv_norm': 1.0 + 0.02 * n(ks[8], (L, MLA_KV_LORA), f32),
        'w_ukv': n(ks[9], (L, MLA_KV_LORA, MLA_HEADS * (MLA_NOPE + MLA_V)), f32) * MLA_KV_LORA ** -0.5,
        'b_forget': 0.1 * n(ks[10], (L, FOX_HEADS), f32),
        'out_norm': 1.0 + 0.02 * n(ks[11], (L, MIX_WIDTH), f32),
        'w_out': n(ks[12], (L, MIX_WIDTH, D), f32) * MIX_WIDTH ** -0.5,
        'norm_ffn': 1.0 + 0.02 * n(ks[13], (L, D), f32),
        'w_ff1': n(ks[14], (L, D, D_FF), f32) * D ** -0.5,
        'w_ff2': n(ks[15], (L, D_FF, D), f32) * D_FF ** -0.5,
        'final_norm': 1.0 + 0.02 * n(ks[16], (D,), f32),
    }

def reference(x, c, w_ada, b_ada, norm_mix, w_in, q_norm, w_uq, kv_norm, w_ukv, b_forget,
              out_norm, w_out, norm_ffn, w_ff1, w_ff2, final_norm):
    B, S, _ = x.shape
    cos, sin = rope_tables(S, MLA_ROPE)
    c_act = jax.nn.silu(c)
    for l in range(DEPTH):
        mod = c_act @ w_ada[l] + b_ada[l]
        sh_a, sc_a, g_a, sh_m, sc_m, g_m = [m[:, None, :] for m in jnp.split(mod, 6, axis=-1)]

        h = rms_norm(x, norm_mix[l]) * (1.0 + sc_a) + sh_a
        p = h @ w_in[l]
        p_cq, p_ckv, p_kr, p_sb, p_fox, p_f = split_sizes(p, IN_SIZES)

        q = (rms_norm(p_cq, q_norm[l]) @ w_uq[l]).reshape(B, S, MLA_HEADS, MLA_NOPE + MLA_ROPE)
        kv = (rms_norm(p_ckv, kv_norm[l]) @ w_ukv[l]).reshape(B, S, MLA_HEADS, MLA_NOPE + MLA_V)
        q_nope = q[..., :MLA_NOPE]
        q_rope = apply_rope(q[..., MLA_NOPE:], cos[None, :, None, :], sin[None, :, None, :])
        k_nope, v_mla = kv[..., :MLA_NOPE], kv[..., MLA_NOPE:]
        k_rope = apply_rope(p_kr, cos[None], sin[None])
        o_mla = mla_attention(q_nope, q_rope, k_nope, k_rope, v_mla)

        q_sb, k_sb, v_sb = [t.reshape(B, S, SB_HEADS, SB_DIM) for t in jnp.split(p_sb, 3, axis=-1)]
        o_sb = stick_breaking_attention(q_sb, k_sb, v_sb)

        q_fx, k_fx, v_fx = [t.reshape(B, S, FOX_HEADS, FOX_DIM) for t in jnp.split(p_fox, 3, axis=-1)]
        log_f = jax.nn.log_sigmoid((p_f + b_forget[l]).astype(jnp.float32))
        o_fx = forgetting_attention(q_fx, k_fx, v_fx, log_f)

        g_mla, g_sb, g_fx = split_sizes(out_norm[l], OUT_SIZES)
        o = jnp.concatenate([head_rms_norm(o_mla, g_mla), head_rms_norm(o_sb, g_sb),
                             head_rms_norm(o_fx, g_fx)], axis=-1)
        x = x + g_a * (o @ w_out[l])

        h = rms_norm(x, norm_ffn[l]) * (1.0 + sc_m) + sh_m
        x = x + g_m * (jnp.square(jax.nn.relu(h @ w_ff1[l])) @ w_ff2[l])
    return rms_norm(x, final_norm)


_drawn_inputs = setup_inputs


def setup_inputs(seed=0):
    import zlib

    import numpy as np

    out = dict(_drawn_inputs(seed))
    spreads = {}
    factors = {'b_ada': 2.997,
     'norm_mix': 8.0,
     'q_norm': 8.0,
     'kv_norm': 8.0,
     'b_forget': 8.0,
     'out_norm': 21.845,
     'norm_ffn': 16.76,
     'final_norm': 24.563}
    for name, (base, spread) in spreads.items():
        noise = np.random.default_rng([zlib.crc32(name.encode()), seed]).standard_normal(out[name].shape)
        drawn = base * np.exp(spread * noise) if base else spread * noise
        out[name] = __import__('jax').numpy.asarray(drawn.astype(out[name].dtype))
    for name, factor in factors.items():
        out[name] = (out[name] * factor).astype(out[name].dtype)
    return out
```

```python
from contextlib import ExitStack

import numpy as np
import concourse.bass as bass
from concourse import mybir

P = 128
D, S, FF = 2048, 256, 8192
EPS = 1e-6
KT = D // P
H, QL, KVL, NOPE, ROPE, VD = 8, 512, 256, 128, 64, 128
DH = 64
CHUNK, ROPE_BASE = 64, 10000.0
MASKED = -1e30
BW = 512
UK = 2
UC = UK * BW
RING = 4
LAG = RING

U_IN = 8 * (KT // UK)
U_UQ, U_UKV = 3 * (QL // P // UK), 4 * (KVL // P // UK)
U_LAT = U_UQ + U_UKV
U_OUT = (D // BW) * (KT // UK)
HALF = FF // 2 // P
U_FF1 = (FF // 2 // BW) * (KT // UK)
U_FF2 = (D // BW) * (HALF // UK)
B_LAT = U_IN
B_OUT = B_LAT + U_LAT
B_FF = B_OUT + U_OUT
UNITS = B_FF + 2 * (U_FF1 + U_FF2)

AC = 1024
CPS = KT * (D // AC)
PRE, ADA = 8, 4
SC_A, SH_A, G_A, SH_M, SC_M, G_M = range(6)
SLICES = (1, 0, 2, 3, 4, 5)

USE_STAT, USE_MOD = 0, 1
USE_IN = 2
USE_LSTAT, USE_LMOD = 10, 11
USE_LAT = 12
USE_ROT, USE_VM, USE_VS = 19, 20, 21
USE_OT = 22
USE_OUT = 24
USE_FSTAT, USE_FMOD = 28, 29
USE_FF1A, USE_GM, USE_FF2A = 30, 38, 39
USE_FF1B, USE_FF2B, USE_END = 43, 51, 55

READY = {use: n + 1 for n, use in enumerate((
    USE_STAT, USE_MOD, USE_LSTAT, USE_LMOD, USE_ROT, USE_VM, USE_VS, USE_OT, USE_OT + 1,
    USE_FSTAT, USE_FMOD, USE_GM, USE_END))}

R_MIX, R_CQ, R_CKV, R_O, R_FFN = 0, 8, 10, 11, 19

C_C, C_B, C_MIX, C_FFN, C_OUT, C_FIN, C_QN, C_KVN, C_BF, C_ONE = np.cumsum(
    [0, KT, 6 * KT, KT, KT, KT, KT, QL // P, KVL // P, 1]).tolist()
C_END = C_ONE + P
K_ID, K_ROT, K_COS, K_SIN, K_FOX, K_SB, K_MLA, K_SEG, K_SEL = np.cumsum(
    [0, P, P, S, S, 3 * P, 3 * P, 3 * P, 3 * P]).tolist()
K_END = K_SEL + H

F32, F32R = mybir.dt.float32, mybir.dt.float32r
ALU, ACT, AX = mybir.AluOpType, mybir.ActivationFunctionType, mybir.AxisListType

SB0, FX0, ML0, HEADS = 0, H, 2 * H, 3 * H
T_CQ, T_CKV, T_KR, T_F, T_SB, T_FX = 0, 4, 6, 7, 8, 20


def hybrid_block(nc, xt_in, cols_in, consts_in, w_ada, weights, out):
    ctx = ExitStack()
    with ctx:
        def sb(name, shape, dt=F32, at=ctx):
            return at.enter_context(nc.sbuf_tensor(name, shape, dt))

        def sem(name):
            return ctx.enter_context(nc.semaphore(name))

        raw = sb("raw", [P, RING, UK, BW])
        w_hi = sb("w_hi", [P, RING, UK, BW], F32R)
        w_lo = sb("w_lo", [P, RING, UK, BW], F32R)
        xT = sb("xT", [P, KT, S])
        ada = sb("ada", [P, ADA, AC])
        accA = sb("accA", [P, D])
        tmp = sb("tmp", [P, 4, S])
        tmp2 = sb("tmp2", [P, 4, S])
        cols = sb("cols", [P, C_END])
        mod = sb("mod", [P, 6, KT])
        c_act = sb("c_act", [P, KT])
        gain = sb("gain", [P, KT])
        rstd = sb("rstd", [P, 2, S])
        small = sb("small", [P, 4 * KT])
        with ExitStack() as r:
            pre = sb("pre", [P, PRE, AC], F32, r)
        with ExitStack() as r:
            q_nope = sb("q_nope", [P, H, S], F32, r)
            k_nope = sb("k_nope", [P, H, S], F32, r)
            q_rope = sb("q_rope", [P, H // 2, S], F32, r)
            rope_raw = sb("rope_raw", [P, H // 2, S], F32, r)
            with ExitStack() as v:
                vT = sb("vT", [P, H, S], F32, v)
            o_tok0 = sb("o_tok0", [P, D], F32, r)
        hT = sb("hT", [P, KT, 2, S], F32R)
        with ExitStack() as r:
            foxA = sb("foxA", [P, S], F32, r)
            foxG = sb("foxG", [P, S], F32, r)
            foxB = sb("foxB", [P, 2, S], F32, r)
            pT = sb("pT", [P, 32, S], F32, r)
            consts = sb("consts", [P, K_END], F32, r)
            v_mla = sb("v_mla", [P, 2, H * VD], F32, r)
            o_tok1 = sb("o_tok1", [P, D], F32, r)
            with ExitStack() as v:
                lat = sb("lat", [P, 6, 2, S], F32R, v)
            zm = sb("zm", [P, 3, 3 * P], F32, r)
            el = sb("el", [P, 2, 3 * P], F32, r)
            stick = sb("stick", [P, 2, 3 * P], F32, r)
        act = sb("act", [P, HALF, 2, S], F32R)
        ssq = sb("ssq", [P, 4, S])
        sq = sb("sq", [P, 4, S])
        accB = o_tok1
        v_sb = pT[:, T_CQ:T_CQ + 4, :].rearrange("p a b -> p (a b)").rearrange("p (t n) -> p t n", t=2)
        v_fx = pT[:, T_SB + 8:T_SB + 12, :].rearrange("p a b -> p (a b)").rearrange("p (t n) -> p t n", t=2)
        o_tok = [o_tok0, o_tok1]
        ones = cols[:, C_ONE:C_ONE + P]
        ident = consts[:, K_ID:K_ID + P]

        def scratch(t):
            return t[:, :, :].rearrange("p a b -> p (a b)")

        probs = [scratch(tmp)[:, i * 384:i * 384 + 384] for i in range(2)]
        probsT = [scratch(tmp2)[:, i * 384:i * 384 + 384] for i in range(2)]
        osq = [scratch(t)[:, 768:1024] for t in (tmp, tmp2)]
        neg_max = small[:, 0:2]
        row = sb("row", [P, HEADS, 2])
        rinv = sb("rinv", [P, HEADS, 2])
        hss = sb("hss", [P, HEADS, 2])
        mx = sb("mx", [P, HEADS, 2])

        ps = [ctx.enter_context(nc.psum_tensor(f"ps{i}", [P, 4, 512], F32)) for i in range(2)]

        ld_cols, ld_x, ld_const, ld_out = sem("ld_cols"), sem("ld_x"), sem("ld_const"), sem("ld_out")
        raw_full = [sem(f"raw_full{i}") for i in range(RING)]
        pre_full = [sem(f"pre_full{i}") for i in range(PRE)]
        ada_full = [sem(f"ada_full{i}") for i in range(ADA)]
        hi_done = sem("hi_done")
        lo_vec, lo_pool = sem("lo_vec"), sem("lo_pool")
        unit_used = sem("unit_used")
        psum_ready = sem("psum_ready")
        psum_free = sem("psum_free")
        tmp_ready = sem("tmp_ready")
        acc_done = sem("acc_done")
        silu_s, mod_s, gain_s = sem("silu_s"), sem("mod_s"), sem("gain_s")
        sum_s = sem("sum_s")
        gated = sem("gated")
        zeroed = sem("zeroed")
        x_new = sem("x_new")
        sq_done, ssq_done = sem("sq_done"), sem("ssq_done")
        ms_s, rt_s, rstd_s = sem("ms_s"), sem("rt_s"), sem("rstd_s")
        t_ready, op_hi, op_lo = sem("t_ready"), sem("op_hi"), sem("op_lo")
        relu2, act_hi, act_lo = sem("relu2"), sem("act_hi"), sem("act_lo")
        lsq = sem("lsq")
        rope_s, rope_c = sem("rope_s"), sem("rope_c")
        va_s = sem("va_s")
        f_s, fa_s, fg_s, fb_s, fm_s = sem("f_s"), sem("fa_s"), sem("fg_s"), sem("fb_s"), sem("fm_s")
        a_sc, a_zm, a_mx, a_ab, a_ex, a_ln = (sem(n) for n in ("a_sc", "a_zm", "a_mx", "a_ab", "a_ex", "a_ln"))
        a_sp, a_scan, a_w, a_p, a_tr, a_pt, a_pv = (
            sem(n) for n in ("a_sp", "a_scan", "a_w", "a_p", "a_tr", "a_pt", "a_pv"))
        a_ri, a_o, a_sq, a_ss, a_n = (sem(n) for n in ("a_ri", "a_o", "a_sq", "a_ss", "a_n"))
        q_sc, fin_s = sem("q_sc"), sem("fin_s")

        block = ctx.enter_context(nc.Block())

        def lo_count(u0, step, it, j):
            return (u0 + j) // 2 + 1 + (step // 2) * it

        def lo_sem(u):
            return lo_vec if u % 2 == 0 else lo_pool

        def head_col(i):
            return VD * (i - ML0) if i >= ML0 else H * VD + DH * i

        @block.sync
        def _(sp):
            def load_unit(u0, step, it, j, fresh=False):
                if not fresh:
                    sp.wait_ge(lo_sem(u0 + j), lo_count(u0 - RING, step, it, j))
                slot = (u0 + j) % RING
                sp.dma_start(raw[:, slot, :, :].rearrange("p k n -> p (k n)"),
                             weights[u0 + j + step * it, :, :]).then_inc(raw_full[slot], 16)

            def load_ada(a0, step, it, j, count):
                sp.wait_ge(acc_done, count + j + step * it)
                slot = (a0 + j) % ADA
                sp.dma_start(ada[:, slot, :], w_ada[a0 + j + step * it, :, :]).then_inc(ada_full[slot], 16)

            sp.dma_start(cols[:, :], cols_in).then_inc(ld_cols, 16)
            for j in range(PRE):
                sp.dma_start(pre[:, j, :], w_ada[j, :, :]).then_inc(pre_full[j], 16)
            sp.dma_start(xT[:, :, :].rearrange("p k t -> p (k t)"), xt_in).then_inc(ld_x, 16)
            with sp.Fori(1, 2 * CPS // PRE) as it:
                for j in range(PRE):
                    sp.wait_ge(acc_done, 3 + j - PRE + PRE * it)
                    sp.dma_start(pre[:, j, :], w_ada[j + PRE * it, :, :]).then_inc(pre_full[j], 16)
            for j in range(RING):
                load_unit(0, 0, 0, j, fresh=True)
            sp.dma_start(consts[:, :], consts_in).then_inc(ld_const, 16)
            with sp.Fori(0, U_IN // RING) as it:
                for j in range(RING):
                    load_ada(2 * CPS, RING, it, j, 2 * CPS + 1)
                    load_unit(LAG, RING, it, j)
            for j in range(U_LAT):
                load_unit(B_LAT + LAG, 0, 0, j)
            with sp.Fori(0, U_OUT // RING) as it:
                for j in range(RING):
                    load_ada(4 * CPS, RING, it, j, 4 * CPS + 2)
                    load_unit(B_OUT + LAG, RING, it, j)
            with sp.Fori(0, U_FF1 // 8) as it:
                for j in range(8):
                    if j % 2 == 0:
                        load_ada(5 * CPS, ADA, it, j // 2, 5 * CPS + 3)
                    load_unit(B_FF + LAG, 8, it, j)
            rest = B_FF + LAG + U_FF1
            with sp.Fori(0, (UNITS - rest) // RING) as it:
                for j in range(RING):
                    load_unit(rest, RING, it, j)
            for j in range(4):
                sp.wait_ge(fin_s, 4 * j + 4)
                src = (tmp, tmp2, sq, ssq)[j]
                sp.dma_start(out[:, 4 * j * S:(4 * j + 4) * S], scratch(src)).then_inc(ld_out, 16)
            sp.wait_ge(ld_out, 64)

        @block.scalar
        def _(sc):
            def hi(u0, step, it, j):
                slot = (u0 + j) % RING
                sc.wait_ge(raw_full[slot], 16 * ((u0 + j) // RING + 1) + (16 * step // RING) * it)
                if u0 + j >= RING:
                    sc.wait_ge(unit_used, u0 + j - RING + 1 + step * it)
                sc.activation(w_hi[:, slot, :, :], raw[:, slot, :, :], ACT.Copy).then_inc(hi_done, 1)

            def copy_low(use, used, step, it):
                sc.wait_ge(unit_used, used + step * it)
                sc.wait_ge(psum_free, use + 2 * it)
                sc.activation(tmp[:, :, :], ps[use % 2][:, :, S:2 * S], ACT.Copy).then_inc(tmp_ready, 1)

            def square(x_count, n, blk, n_blk, n_sq):
                sc.wait_ge(x_new, x_count + n)
                if n_sq:
                    sc.wait_ge(ssq_done, n_blk)
                sc.activation(sq[:, :, :], xT[:, bass.ds(blk, 4), :], ACT.Square).then_inc(sq_done, 1)

            def root(n, halves=1):
                sc.wait_ge(ms_s, n)
                sc.activation(rstd[:, 0:halves, :], rstd[:, 0:halves, :], ACT.Sqrt).then_inc(rt_s, 1)

            def operand_hi(n, dst, bias):
                sc.wait_ge(t_ready, n + 1)
                t = tmp[:, 2 * (n % 2):2 * (n % 2) + 2, :]
                if bias is None:
                    sc.activation(dst[:, :, 0, :], t, ACT.Copy).then_inc(op_hi, 1)
                else:
                    sc.activation(dst[:, 0, 0, :], t[:, 0, :], ACT.Identity, bias=bias[:, 0:1])
                    sc.activation(dst[:, 1, 0, :], t[:, 1, :], ACT.Identity, bias=bias[:, 1:2]).then_inc(op_hi, 1)

            sc.wait_ge(ld_cols, 16)
            sc.activation(c_act[:, :], cols[:, C_C:C_C + KT], ACT.Exp, scale=-1.0).then_inc(silu_s, 1)
            sc.wait_ge(ld_x, 16)
            for b in range(4):
                if b:
                    sc.wait_ge(ssq_done, b)
                sc.activation(sq[:, :, :], xT[:, 4 * b:4 * b + 4, :], ACT.Square).then_inc(sq_done, 1)
            root(1)
            for j in range(RING):
                hi(0, 0, 0, j)
            for j in range(8):
                if j == 0:
                    sc.wait_ge(mod_s, 2)
                operand_hi(R_MIX + j, hT[:, 2 * j:2 * j + 2, :, :], mod[:, SH_A, 2 * j:2 * j + 2])
            with sc.Fori(0, 4) as it:
                for b in range(2):
                    for j in range(8):
                        hi(LAG, 16, it, 8 * b + j)
                    copy_low(USE_IN + b, 8 * b + 8, 16, it)
            sc.wait_ge(psum_free, USE_LSTAT)
            for i, n in ((0, 4), (1, 2)):
                if i:
                    sc.wait_ge(lsq, 1)
                sc.activation(tmp2[:, 0:n, :], pT[:, T_CQ + 4 * i:T_CQ + 4 * i + n, :],
                              ACT.Square).then_inc(sq_done, 1)
            root(2, halves=2)
            for n in range(3):
                operand_hi(R_CQ + n, lat[:, 2 * n:2 * n + 2, :, :], None)
            fx = foxB[0:H, 0, :]
            fl = foxB[0:H, 1, :]
            sc.wait_ge(f_s, 1)
            sc.activation(fl, fx, ACT.Abs).then_inc(f_s, 1)
            sc.wait_ge(f_s, 2)
            sc.activation(fl, fl, ACT.Exp, scale=-1.0).then_inc(f_s, 1)
            sc.wait_ge(f_s, 3)
            sc.activation(fl, fl, ACT.Ln, bias=cols[0:H, C_ONE:C_ONE + 1]).then_inc(f_s, 1)
            sc.wait_ge(f_s, 6)
            sc.activation(foxG[32:32 + H, :], foxA[0:H, :], ACT.Copy, scale=-1.0).then_inc(fg_s, 1)
            ends = [1, 3, 5, 6, 7, 8, 9]
            for n, e in enumerate(ends):
                for u in range(LAG if n == 0 else ends[n - 1] + 1 + LAG, e + 1 + LAG):
                    hi(B_LAT, 0, 0, u)
                copy_low(USE_LAT + n, B_LAT + e + 1, 0, 0)
            sc.wait_ge(psum_ready, READY[USE_VM])
            sc.activation(v_mla[:, 0, :], ps[USE_VM % 2][:, 0:2, :].rearrange("p a b -> p (a b)"),
                          ACT.Copy).then_inc(va_s, 1)
            sc.wait_ge(psum_ready, READY[USE_VS])
            sc.activation(v_sb, ps[USE_VS % 2][:, 0:2, :], ACT.Copy).then_inc(va_s, 1)

            def soft_parts(i):
                e = el[:, i % 2, :]
                sc.wait_ge(a_zm, i + 1)
                if i >= 2:
                    sc.wait_ge(a_scan, i - 1)
                sc.activation(e, zm[:, i % 3, :], ACT.Abs).then_inc(a_ab, 1)
                sc.wait_ge(a_ab, i + 1)
                sc.activation(e, e, ACT.Exp, scale=-1.0).then_inc(a_ex, 1)
                sc.wait_ge(a_ex, i + 1)
                sc.activation(e, e, ACT.Ln, bias=cols[:, C_ONE:C_ONE + 1]).then_inc(a_ln, 1)

            def weights_of(i):
                p = probs[i % 2]
                if i >= 2:
                    sc.wait_ge(a_tr, i - 1)
                if i < FX0:
                    sc.wait_ge(a_w, i + 1)
                    sc.activation(p, zm[:, i % 3, :], ACT.Exp).then_inc(a_p, 1)
                else:
                    sc.wait_ge(a_mx, 2 * (i - FX0) + 2)
                    sc.activation(p[:, 0:P], zm[:, i % 3, 0:P], ACT.Exp, bias=mx[:, i, 0:1],
                                  accum_out=row[:, i, 0:1])
                    sc.activation(p[:, P:3 * P], zm[:, i % 3, P:3 * P], ACT.Exp, bias=mx[:, i, 1:2],
                                  accum_out=row[:, i, 1:2]).then_inc(a_p, 1)

            def copy_pt(i):
                sc.wait_ge(a_tr, i + 1)
                if i >= 2:
                    sc.wait_ge(a_pv, i - 1)
                sc.activation(probsT[i % 2], ps[0][:, 2 + i % 2, 0:3 * P], ACT.Copy).then_inc(a_pt, 1)

            for t in range(HEADS + 3):
                if t < FX0:
                    soft_parts(t)
                if 0 <= t - 2 < HEADS:
                    weights_of(t - 2)
                if 0 <= t - 3 < HEADS:
                    copy_pt(t - 3)
            sc.wait_ge(ms_s, 3)
            sc.activation(hss[:, :, :], hss[:, :, :], ACT.Sqrt).then_inc(rt_s, 1)
            for j in range(8):
                operand_hi(R_O + j, hT[:, 2 * j:2 * j + 2, :, :], None)
            with sc.Fori(0, 2) as it:
                for b in range(2):
                    for j in range(8):
                        hi(B_OUT + LAG, 16, it, 8 * b + j)
                    copy_low(USE_OUT + b, B_OUT + 8 * b + 8, 16, it)
                    square(b + 1, 2 * it, 4 * b + 8 * it, 4 + b + 2 * it, True)
            root(4)
            for j in range(8):
                if j == 0:
                    sc.wait_ge(mod_s, 4)
                operand_hi(R_FFN + j, hT[:, 2 * j:2 * j + 2, :, :], mod[:, SH_M, 2 * j:2 * j + 2])

            for half in range(2):
                base = B_FF + half * (U_FF1 + U_FF2)
                use1 = (USE_FF1A, USE_FF1B)[half]
                with sc.Fori(0, 4) as it:
                    for b in range(2):
                        for j in range(8):
                            hi(base + LAG, 16, it, 8 * b + j)
                        copy_low(use1 + b, base + 8 * b + 8, 16, it)
                        sc.wait_ge(relu2, 8 * half + b + 1 + 2 * it)
                        sc.activation(act[:, bass.ds(4 * b + 8 * it, 4), 0, :], tmp2[:, :, :],
                                      ACT.Copy).then_inc(act_hi, 1)
                use2 = (USE_FF2A, USE_FF2B)[half]

                def down(it, last=False):
                    for b in range(2):
                        for j in range(16):
                            if not (last and b == 1 and j >= 16 - LAG):
                                hi(base + U_FF1 + LAG, 32, it, 16 * b + j)
                        copy_low(use2 + b, base + U_FF1 + 16 * b + 16, 32, it)
                        if half == 1:
                            square(8 + b + 1, 2 * it, 4 * b + 8 * it, 8 + b + 2 * it, True)

                if half == 0:
                    with sc.Fori(0, 2) as it:
                        down(it)
                else:
                    down(0)
                    down(1, last=True)
            root(5)

        @block.gpsimd
        def _(gp):
            def lo(u0, step, it, j):
                if (u0 + j) % 2 == 1:
                    slot = (u0 + j) % RING
                    gp.wait_ge(hi_done, u0 + j + 1 + step * it)
                    gp.tensor_tensor(w_lo[:, slot, :, :], raw[:, slot, :, :],
                                     w_hi[:, slot, :, :].bitcast(F32), ALU.subtract).then_inc(lo_pool, 1)

            def gate(n, n_it, blk, g, g_it):
                gp.wait_ge(sum_s, n + n_it)
                gp.tensor_tensor(tmp2[:, :, :], tmp2[:, :, :],
                                 mod[:, g, bass.ds(g_it, 4)].unsqueeze(2).to_broadcast([P, 4, S]),
                                 ALU.mult).then_inc(gated, 1)
                gp.wait_ge(gated, n + n_it)
                x = xT[:, bass.ds(blk, 4), :]
                gp.tensor_tensor(x, x, tmp2[:, :, :], ALU.add).then_inc(x_new, 1)

            def add_squares(n):
                gp.wait_ge(sq_done, n)
                gp.tensor_tensor(ssq[:, :, :], ssq[:, :, :], sq[:, :, :], ALU.add).then_inc(ssq_done, 1)

            gp.memset(ssq[:, :, :], 0.0).then_inc(zeroed, 1)
            gp.wait_ge(zeroed, 1)
            for b in range(4):
                add_squares(b + 1)
            for j in range(RING):
                lo(0, 0, 0, j)
            with gp.Fori(0, 4) as it:
                for j in range(16):
                    lo(LAG, 16, it, j)
            gp.wait_ge(psum_free, USE_LSTAT)
            gp.memset(foxA[:, :], 0.0).then_inc(fm_s, 1)
            gp.memset(foxG[:, :], 0.0).then_inc(fm_s, 1)
            gp.wait_ge(fm_s, 2)
            gp.memset(foxA[32:32 + H, :], 1.0).then_inc(fm_s, 1)
            gp.wait_ge(fm_s, 3)
            gp.memset(foxG[0:H, :], 1.0).then_inc(fm_s, 1)
            gp.wait_ge(fm_s, 4)
            for j in range(LAG, U_LAT + LAG):
                lo(B_LAT, 0, 0, j)

            def stick_weight(i):
                gp.wait_ge(a_scan, i + 1)
                z = zm[:, i % 3, :]
                gp.tensor_tensor(z, z, stick[:, i % 2, :], ALU.subtract).then_inc(a_w, 1)

            def fox_operand(i):
                n = i - FX0
                if n >= 2:
                    gp.wait_ge(a_sc, i - 1)
                gp.tensor_scalar(foxB[:, n % 2, :], foxG[:, :], consts[:, K_SEL + n:K_SEL + n + 1], None,
                                 ALU.mult).then_inc(fb_s, 1)

            def out_square(i):
                d = VD if i >= ML0 else DH
                gp.wait_ge(a_o, i + 1)
                if i >= 2:
                    gp.wait_ge(a_ss, i - 1)
                for q in range(2):
                    o = o_tok[q][:, head_col(i):head_col(i) + d]
                    ins = gp.tensor_tensor(osq[i % 2][:, q * d:q * d + d], o, o, ALU.mult)
                ins.then_inc(a_sq, 1)

            for t in range(HEADS + 5):
                if t == FX0 - 2:
                    gp.wait_ge(fg_s, 1)
                    gp.wait_ge(fm_s, 4)
                if FX0 <= t + 2 < ML0:
                    fox_operand(t + 2)
                if 0 <= t - 1 < FX0:
                    stick_weight(t - 1)
                if 0 <= t - 4 < HEADS:
                    out_square(t - 4)
            gp.wait_ge(a_n, 4)
            gp.memset(ssq[:, :, :], 0.0).then_inc(zeroed, 1)
            gp.wait_ge(zeroed, 2)
            with gp.Fori(0, 2) as it:
                for b in range(2):
                    for j in range(8):
                        lo(B_OUT + LAG, 16, it, 8 * b + j)
                    gate(b + 1, 2 * it, 4 * b + 8 * it, G_A, 4 * b + 8 * it)
                    add_squares(6 + b + 1 + 2 * it)
            gp.wait_ge(psum_ready, READY[USE_FSTAT])
            gp.memset(ssq[:, :, :], 0.0).then_inc(zeroed, 1)
            gp.wait_ge(zeroed, 3)
            for half in range(2):
                base = B_FF + half * (U_FF1 + U_FF2)
                with gp.Fori(0, 4) as it:
                    for j in range(16):
                        lo(base + LAG, 16, it, j)

                def down(it, last=False):
                    for b in range(2):
                        for j in range(16):
                            if not (last and b == 1 and j >= 16 - LAG):
                                lo(base + U_FF1 + LAG, 32, it, 16 * b + j)
                        gate(4 + 4 * half + b + 1, 2 * it, 4 * b + 8 * it, G_M, 4 * b + 8 * it)
                        if half == 1:
                            add_squares(10 + b + 1 + 2 * it)

                if half == 0:
                    with gp.Fori(0, 2) as it:
                        down(it)
                else:
                    down(0)
                    down(1, last=True)

        @block.vector
        def _(ve):
            def lo(u0, step, it, j):
                if (u0 + j) % 2 == 0:
                    slot = (u0 + j) % RING
                    ve.wait_ge(hi_done, u0 + j + 1 + step * it)
                    ve.tensor_tensor(w_lo[:, slot, :, :], raw[:, slot, :, :],
                                     w_hi[:, slot, :, :].bitcast(F32), ALU.subtract).then_inc(lo_vec, 1)

            def add_chunk(acc, a0, count, step, it, j):
                src, full, ring, own = (pre, pre_full, PRE, 0) if a0 < 2 * CPS else (ada, ada_full, ADA, 2 * CPS)
                slot = (a0 + j) % ring
                ve.wait_ge(full[slot], 16 * ((a0 + j - own) // ring + 1) + (16 * step // ring) * it)
                ve.wait_ge(acc_done, count + a0 + j + step * it)
                n = (a0 + j) % 2
                dst = acc[:, n * AC:(n + 1) * AC]
                kt = a0 % CPS // 2 + j // 2 + (step // 2) * it
                ve.scalar_tensor_tensor(out=dst, in0=src[:, slot, :], scalar=c_act[:, bass.ds(kt, 1)],
                                        in1=dst, op0=ALU.mult, op1=ALU.add).then_inc(acc_done, 1)

            def mean(use, bank, half, width):
                return ve.tensor_scalar(rstd[:, half, :], ps[use % 2][:, bank, 0:S], 1.0 / width, EPS,
                                        ALU.mult, ALU.add)

            def invert(n, done, halves=1):
                ve.wait_ge(rt_s, n)
                ve.reciprocal(rstd[:, 0:halves, :], rstd[:, 0:halves, :]).then_inc(rstd_s, 1)
                ve.wait_ge(rstd_s, done)

            def read_mod(use, bank, g):
                src = C_B + KT * SLICES[g]
                return ve.tensor_tensor(mod[:, g, :], ps[use % 2][:, bank, 0:KT], cols[:, src:src + KT], ALU.add)

            def make_gain(g, c):
                ve.scalar_tensor_tensor(out=gain[:, :], in0=mod[:, g, :], scalar=1.0, in1=cols[:, c:c + KT],
                                        op0=ALU.add, op1=ALU.mult).then_inc(gain_s, 1)

            def slot_of(n):
                return tmp[:, 2 * (n % 2):2 * (n % 2) + 2, :]

            def scaled_pair(n, src, g, half):
                if n >= 2:
                    ve.wait_ge(op_lo, n - 1)
                for k in range(2):
                    ins = ve.scalar_tensor_tensor(out=slot_of(n)[:, k, :], in0=src[:, k, :], scalar=g[:, k:k + 1],
                                                  in1=rstd[:, half, :], op0=ALU.mult, op1=ALU.mult)
                ins.then_inc(t_ready, 1)

            def operand_lo(n, dst, bias):
                ve.wait_ge(op_hi, n + 1)
                if bias is None:
                    ve.tensor_tensor(dst[:, :, 1, :], slot_of(n), dst[:, :, 0, :].bitcast(F32),
                                     ALU.subtract).then_inc(op_lo, 1)
                else:
                    for k in range(2):
                        ins = ve.scalar_tensor_tensor(out=dst[:, k, 1, :], in0=slot_of(n)[:, k, :],
                                                      scalar=bias[:, k:k + 1], in1=dst[:, k, 0, :].bitcast(F32),
                                                      op0=ALU.add, op1=ALU.subtract)
                    ins.then_inc(op_lo, 1)

            def modulated_norm(r0, shift):
                for j in range(9):
                    if j < 8:
                        scaled_pair(r0 + j, xT[:, 2 * j:2 * j + 2, :], gain[:, 2 * j:2 * j + 2], 0)
                    if j:
                        i = j - 1
                        operand_lo(r0 + i, hT[:, 2 * i:2 * i + 2, :, :], mod[:, shift, 2 * i:2 * i + 2])

            def sum_halves(dst, use, n_use, e, n_e, it, done):
                ve.wait_ge(tmp_ready, e + 1 + n_e * it)
                ve.tensor_tensor(dst, ps[use % 2][:, :, 0:S], tmp[:, :, :], ALU.add).then_inc(done, 1)

            ve.memset(accA[:, :], 0.0).then_inc(acc_done, 1)
            ve.memset(accB[:, :], 0.0).then_inc(acc_done, 1)
            ve.wait_ge(silu_s, 1)
            den = small[:, 0:KT]
            ve.tensor_scalar(den, c_act[:, :], 1.0, None, ALU.add).then_inc(silu_s, 1)
            ve.wait_ge(silu_s, 2)
            ve.reciprocal(den, den).then_inc(silu_s, 1)
            ve.wait_ge(silu_s, 3)
            ve.tensor_tensor(c_act[:, :], cols[:, C_C:C_C + KT], den, ALU.mult).then_inc(silu_s, 1)
            ve.wait_ge(silu_s, 4)
            with ve.Fori(0, CPS // PRE) as it:
                for j in range(PRE):
                    add_chunk(accA, 0, 1, PRE, it, j)
            ve.wait_ge(psum_ready, READY[USE_STAT])
            mean(USE_STAT, 0, 0, D).then_inc(ms_s, 1)
            read_mod(USE_STAT, 1, SC_A).then_inc(mod_s, 1)
            ve.wait_ge(ms_s, 1)
            ve.wait_ge(mod_s, 1)
            make_gain(SC_A, C_MIX)
            invert(1, 1)
            with ve.Fori(0, CPS // PRE) as it:
                for j in range(PRE):
                    add_chunk(accB, CPS, 1, PRE, it, j)
            ve.wait_ge(gain_s, 1)
            ve.sem_inc(psum_free, 1)
            for j in range(RING):
                lo(0, 0, 0, j)
            ve.wait_ge(psum_ready, READY[USE_MOD])
            read_mod(USE_MOD, 0, SH_A).then_inc(mod_s, 1)
            ve.wait_ge(mod_s, 2)
            ve.sem_inc(psum_free, 1)
            ve.memset(accA[:, :], 0.0).then_inc(acc_done, 1)
            ve.memset(accB[:, :], 0.0).then_inc(acc_done, 1)
            modulated_norm(R_MIX, SH_A)

            for half, acc in ((0, accA), (1, accB)):
                with ve.Fori(0, 2) as it:
                    for b in range(2):
                        for j in range(8 * b, 8 * b + 8):
                            lo(LAG + U_IN // 2 * half, 16, it, j)
                            add_chunk(acc, (2 + half) * CPS, 3, 16, it, j)
                        sum_halves(pT[:, bass.ds(16 * half + 4 * b + 8 * it, 4), :],
                                   USE_IN + b, 2, 4 * half + b, 2, it, psum_free)

            ve.wait_ge(psum_ready, READY[USE_LSTAT])
            mean(USE_LSTAT, 0, 0, QL)
            mean(USE_LSTAT, 1, 1, KVL).then_inc(ms_s, 1)
            ve.wait_ge(ms_s, 2)
            ve.sem_inc(psum_free, 1)
            invert(2, 2, halves=2)
            for n in range(4):
                if n < 3:
                    g = C_QN + 2 * n
                    scaled_pair(R_CQ + n, pT[:, T_CQ + 2 * n:T_CQ + 2 * n + 2, :], cols[:, g:g + 2], n // 2)
                if n:
                    operand_lo(R_CQ + n - 1, lat[:, 2 * n - 2:2 * n, :, :], None)
            ve.wait_ge(psum_ready, READY[USE_LMOD])
            read_mod(USE_LMOD, 0, G_A).then_inc(mod_s, 1)
            read_mod(USE_LMOD, 1, SH_M).then_inc(mod_s, 1)
            ve.wait_ge(mod_s, 4)
            ve.sem_inc(psum_free, 1)
            fx, fl = foxB[0:H, 0, :], foxB[0:H, 1, :]
            ve.tensor_scalar(fx, pT[0:H, T_F, :], cols[0:H, C_BF:C_BF + 1], None, ALU.add).then_inc(f_s, 1)
            ve.tensor_scalar(pT[:, T_SB:T_SB + 4, :], pT[:, T_SB:T_SB + 4, :], DH ** -0.5, None,
                             ALU.mult).then_inc(q_sc, 1)
            ve.tensor_scalar(pT[:, T_FX:T_FX + 4, :], pT[:, T_FX:T_FX + 4, :], DH ** -0.5, None,
                             ALU.mult).then_inc(q_sc, 1)
            ve.wait_ge(f_s, 4)
            ve.scalar_tensor_tensor(out=fx, in0=fx, scalar=0.0, in1=fl, op0=ALU.min,
                                    op1=ALU.subtract).then_inc(f_s, 1)
            ve.wait_ge(f_s, 5)
            ve.wait_ge(fm_s, 2)
            ve.tensor_tensor_scan(foxA[0:H, :], consts[0:H, K_SEG:K_SEG + 1].to_broadcast([H, S]), fx, 0.0, ALU.mult, ALU.add).then_inc(f_s, 1)
            ends = [1, 3, 5, 6, 7, 8, 9]
            dests = [q_nope[:, 0:4, :], q_nope[:, 4:8, :], rope_raw[:, :, :], k_nope[:, 0:4, :],
                     k_nope[:, 4:8, :], vT[:, 0:4, :], vT[:, 4:8, :]]
            for n, e in enumerate(ends):
                for u in range(LAG if n == 0 else ends[n - 1] + 1 + LAG, e + 1 + LAG):
                    lo(B_LAT, 0, 0, u)
                sum_halves(dests[n], USE_LAT + n, 0, 8 + n, 0, 0, psum_free)
            cos, sin = consts[:, K_COS:K_COS + S], consts[:, K_SIN:K_SIN + S]
            cos4 = cos.unsqueeze(1).to_broadcast([P, 4, S])
            sin4 = sin.unsqueeze(1).to_broadcast([P, 4, S])
            rot = ps[USE_ROT % 2]
            ve.tensor_tensor(q_rope[:, :, :], rope_raw[:, :, :], cos4, ALU.mult).then_inc(rope_s, 1)
            ve.tensor_tensor(rstd[:, 0, :], pT[:, T_KR, :], cos, ALU.mult).then_inc(rope_s, 1)
            ve.wait_ge(psum_ready, READY[USE_ROT])
            ve.tensor_tensor(tmp2[:, :, :], rot[:, 0:2, :].rearrange("p b (h t) -> p (b h) t", h=2), sin4,
                             ALU.mult).then_inc(rope_s, 1)
            ve.tensor_tensor(rstd[:, 1, :], rot[:, 2, 0:S], sin, ALU.mult).then_inc(rope_s, 1)
            ve.wait_ge(rope_s, 4)
            ve.sem_inc(psum_free, 1)
            ve.tensor_tensor(q_rope[:, :, :], q_rope[:, :, :], tmp2[:, :, :], ALU.add).then_inc(rope_c, 1)
            ve.tensor_tensor(pT[:, T_KR, :], rstd[:, 0, :], rstd[:, 1, :], ALU.add).then_inc(rope_c, 1)
            ve.wait_ge(va_s, 1)
            ve.tensor_copy(v_mla[:, 1, :], ps[USE_VM % 2][:, 2:4, :].rearrange("p a b -> p (a b)"))\
                .then_inc(psum_free, 1)
            ve.wait_ge(va_s, 2)
            ve.tensor_copy(v_fx, ps[USE_VS % 2][:, 2:4, :]).then_inc(psum_free, 1)

            def masked_scores(i):
                s = ps[0][:, i % 2, 0:3 * P]
                z = zm[:, i % 3, :]
                ve.wait_ge(a_sc, i + 1)
                if i >= 3:
                    ve.wait_ge(a_p, i - 2)
                if i >= ML0:
                    ve.scalar_tensor_tensor(out=z, in0=s, scalar=(NOPE + ROPE) ** -0.5,
                                            in1=consts[:, K_MLA:K_MLA + 3 * P], op0=ALU.mult,
                                            op1=ALU.add).then_inc(a_zm, 1)
                else:
                    k = K_SB if i < FX0 else K_FOX
                    ve.tensor_tensor(z, s, consts[:, k:k + 3 * P], ALU.add).then_inc(a_zm, 1)
                if i >= FX0:
                    ve.wait_ge(a_zm, i + 1)
                    ve.tensor_reduce(mx[:, i, 0:1], z[:, 0:P], AX.X, ALU.max, negate=True).then_inc(a_mx, 1)
                    ve.tensor_reduce(mx[:, i, 1:2], z[:, P:3 * P], AX.X, ALU.max, negate=True).then_inc(a_mx, 1)

            def stick_sums(i):
                e, z, r = el[:, i % 2, :], zm[:, i % 3, :], stick[:, i % 2, :]
                ve.wait_ge(a_ln, i + 1)
                ve.scalar_tensor_tensor(out=e, in0=z, scalar=0.0, in1=e, op0=ALU.max,
                                        op1=ALU.add).then_inc(a_sp, 1)
                ve.wait_ge(a_sp, i + 1)
                if i >= 2:
                    ve.wait_ge(a_w, i - 1)
                ve.tensor_tensor_scan(r[:, ::-1], consts[:, K_SEG:K_SEG + 3 * P][:, ::-1], e[:, ::-1], 0.0,
                                      ALU.mult, ALU.add).then_inc(a_scan, 1)

            def read_output(i):
                d, c = (VD if i >= ML0 else DH), head_col(i)
                ve.wait_ge(a_pv, i + 1)
                if i >= FX0:
                    ve.reciprocal(rinv[:, i, :], row[:, i, :]).then_inc(a_ri, 1)
                    ve.wait_ge(a_ri, i - FX0 + 1)
                for q in range(2):
                    o, src = o_tok[q][:, c:c + d], ps[1][:, i % 2, q * d:(q + 1) * d]
                    if i >= FX0:
                        ins = ve.tensor_scalar(o, src, rinv[:, i, q:q + 1], None, ALU.mult)
                    else:
                        ins = ve.tensor_copy(o, src)
                ins.then_inc(a_o, 1)

            def sum_squares(i):
                d = VD if i >= ML0 else DH
                ve.wait_ge(a_sq, i + 1)
                ve.tensor_reduce(hss[:, i, :], osq[i % 2][:, 0:2 * d].rearrange("p (q d) -> p q d", q=2),
                                 AX.X, ALU.add).then_inc(a_ss, 1)

            for t in range(HEADS + 5):
                if t < HEADS:
                    masked_scores(t)
                if 0 <= t - 1 < FX0:
                    stick_sums(t - 1)
                if 0 <= t - 4 < HEADS:
                    read_output(t - 4)
                if 0 <= t - 5 < HEADS:
                    sum_squares(t - 5)
            ve.wait_ge(a_ss, HEADS)
            ve.tensor_scalar(hss[:, 0:ML0, :], hss[:, 0:ML0, :], 1.0 / DH, EPS, ALU.mult, ALU.add)
            ve.tensor_scalar(hss[:, ML0:HEADS, :], hss[:, ML0:HEADS, :], 1.0 / VD, EPS, ALU.mult,
                             ALU.add).then_inc(ms_s, 1)
            ve.wait_ge(rt_s, 3)
            ve.reciprocal(hss[:, :, :], hss[:, :, :]).then_inc(a_ri, 1)
            ve.wait_ge(a_ri, HEADS - FX0 + 1)
            for first, n, d in ((ML0, H, VD), (0, ML0, DH)):
                for q in range(2):
                    o = o_tok[q][:, head_col(first):head_col(first) + n * d].rearrange("p (h d) -> p h d", d=d)
                    ve.tensor_tensor(o, o, hss[:, first:first + n, q].unsqueeze(2).to_broadcast([P, n, d]),
                                     ALU.mult).then_inc(a_n, 1)
            for j in range(9):
                if j < 8:
                    use = USE_OT + j // 4
                    ve.wait_ge(psum_ready, READY[use])
                    ve.wait_ge(op_lo, R_O + j - 1)
                    ins = ve.tensor_tensor(slot_of(R_O + j),
                                           ps[use % 2][:, j % 4, :].rearrange("p (k t) -> p k t", k=2),
                                           cols[:, C_OUT + 2 * j:C_OUT + 2 * j + 2].unsqueeze(2).to_broadcast([P, 2, S]),
                                           ALU.mult)
                    ins.then_inc(t_ready, 1)
                    if j % 4 == 3:
                        ve.wait_ge(t_ready, R_O + j + 1)
                        ve.sem_inc(psum_free, 1)
                if j:
                    operand_lo(R_O + j - 1, hT[:, 2 * j - 2:2 * j, :, :], None)

            ve.memset(accA[:, :], 0.0).then_inc(acc_done, 1)
            ve.wait_ge(acc_done, 4 * CPS + 5)
            with ve.Fori(0, 2) as it:
                for b in range(2):
                    for j in range(8 * b, 8 * b + 8):
                        lo(B_OUT + LAG, 16, it, j)
                        add_chunk(accA, 4 * CPS, 4, 16, it, j)
                    sum_halves(tmp2[:, :, :], USE_OUT + b, 2, 15 + b, 2, it, sum_s)
                    ve.wait_ge(sum_s, b + 1 + 2 * it)
                    ve.sem_inc(psum_free, 1)
            ve.wait_ge(psum_ready, READY[USE_FMOD])
            mean(USE_FSTAT, 0, 0, D).then_inc(ms_s, 1)
            read_mod(USE_FMOD, 0, SC_M).then_inc(mod_s, 1)
            ve.wait_ge(ms_s, 4)
            ve.wait_ge(mod_s, 5)
            ve.sem_inc(psum_free, 2)
            make_gain(SC_M, C_FFN)
            ve.wait_ge(gain_s, 2)
            invert(4, 3)
            modulated_norm(R_FFN, SH_M)
            ve.memset(accA[:, :], 0.0).then_inc(acc_done, 1)
            ve.wait_ge(acc_done, 5 * CPS + 6)

            for half in range(2):
                base = B_FF + half * (U_FF1 + U_FF2)
                use1, e1 = ((USE_FF1A, 19), (USE_FF1B, 31))[half]
                if half == 1:
                    ve.wait_ge(x_new, 8)
                with ve.Fori(0, 4) as it:
                    for b in range(2):
                        for j in range(8 * b, 8 * b + 8):
                            lo(base + LAG, 16, it, j)
                            if half == 0 and j % 2 == 1:
                                add_chunk(accA, 5 * CPS, 5, 8, it, j // 2)
                        sum_halves(tmp2[:, :, :], use1 + b, 2, e1 + b, 2, it, psum_free)
                        ve.wait_ge(psum_free, use1 + b + 1 + 2 * it)
                        ve.scalar_tensor_tensor(out=tmp2[:, :, :], in0=tmp2[:, :, :], scalar=0.0,
                                                in1=tmp2[:, :, :], op0=ALU.max, op1=ALU.mult).then_inc(relu2, 1)
                        blk = bass.ds(4 * b + 8 * it, 4)
                        ve.wait_ge(act_hi, 8 * half + b + 1 + 2 * it)
                        ve.tensor_tensor(act[:, blk, 1, :], tmp2[:, :, :], act[:, blk, 0, :].bitcast(F32),
                                         ALU.subtract).then_inc(act_lo, 1)
                use2, e2 = ((USE_FF2A, 27), (USE_FF2B, 39))[half]
                if half == 0:
                    ve.wait_ge(psum_ready, READY[USE_GM])
                    read_mod(USE_GM, 0, G_M).then_inc(mod_s, 1)
                    ve.wait_ge(mod_s, 6)
                    ve.sem_inc(psum_free, 1)

                def down(it, last=False):
                    for b in range(2):
                        for j in range(16):
                            if not (last and b == 1 and j >= 16 - LAG):
                                lo(base + U_FF1 + LAG, 32, it, 16 * b + j)
                        if half == 0:
                            ve.wait_ge(x_new, 4 + b + 2 * it)
                        sum_halves(tmp2[:, :, :], use2 + b, 2, e2 + b, 2, it, sum_s)
                        ve.wait_ge(sum_s, 4 + 4 * half + b + 1 + 2 * it)
                        ve.sem_inc(psum_free, 1)

                if half == 0:
                    with ve.Fori(0, 2) as it:
                        down(it)
                else:
                    down(0)
                    down(1, last=True)
            ve.wait_ge(psum_ready, READY[USE_END])
            mean(USE_END, 0, 0, D).then_inc(ms_s, 1)
            invert(5, 4)
            for k in range(KT):
                dst = (tmp, tmp2, sq, ssq)[k // 4]
                ve.scalar_tensor_tensor(out=dst[:, k % 4, :], in0=xT[:, k, :], scalar=cols[:, C_FIN + k:C_FIN + k + 1],
                                        in1=rstd[:, 0, :], op0=ALU.mult, op1=ALU.mult).then_inc(fin_s, 1)

        @block.tensor
        def _(pe):
            def take(use, n_use=0, it=0):
                if use >= 2:
                    pe.wait_ge(psum_free, use - 1 + n_use * it)

            def unit(u0, step, it, j, out_set, rhs, kt0, ready, first, last):
                slot = (u0 + j) % RING
                pe.wait_ge(*ready)
                pe.wait_ge(hi_done, u0 + j + 1 + step * it)
                for k in range(UK):
                    for n in range(4):
                        pe.matmul(out_set[:, n, :], w_hi[:, slot, k, n * P:(n + 1) * P], rhs[:, kt0 + k, :, :],
                                  start=first and k == 0, stop=False)
                pe.wait_ge(lo_sem(u0 + j), lo_count(u0, step, it, j))
                for k in range(UK):
                    for n in range(4):
                        ins = pe.matmul(out_set[:, n, 0:S], w_lo[:, slot, k, n * P:(n + 1) * P],
                                        rhs[:, kt0 + k, 0, :], start=False, stop=last and k == UK - 1)
                ins.then_inc(unit_used, 1)

            def product(u0, step, it, j0, units, use, n_use, rhs, kt0, ready):
                take(use, n_use, it)
                for j in range(units):
                    unit(u0, step, it, j0 + j, ps[use % 2], rhs, kt0 + UK * j, ready(j), j == 0, j == units - 1)

            def column_sums(use, bank, acc):
                for k in range(KT):
                    ins = pe.matmul(ps[use % 2][:, bank, k:k + 1], acc[:, k * P:(k + 1) * P], ones[:, 0:1],
                                    start=True, stop=True)
                return ins

            def token_sums(use, bank, src, n):
                for k in range(n):
                    ins = pe.matmul(ps[use % 2][:, bank, 0:S], ones, src[:, k, :], start=(k == 0), stop=(k == n - 1))
                return ins

            pe.wait_ge(ld_cols, 16)
            pe.wait_ge(ssq_done, 4)
            token_sums(USE_STAT, 0, ssq, 4)
            pe.wait_ge(acc_done, CPS + 2)
            column_sums(USE_STAT, 1, accA).then_inc(psum_ready, 1)
            pe.wait_ge(acc_done, 2 * CPS + 2)
            column_sums(USE_MOD, 0, accB).then_inc(psum_ready, 1)
            with pe.Fori(0, 4) as it:
                for b in range(2):
                    product(0, 16, it, 8 * b, 8, USE_IN + b, 2, hT, 0, lambda j: (op_lo, R_MIX + j + 1))
            take(USE_LSTAT)
            pe.wait_ge(sq_done, 5)
            token_sums(USE_LSTAT, 0, tmp2, 4).then_inc(lsq, 1)
            pe.wait_ge(sq_done, 6)
            token_sums(USE_LSTAT, 1, tmp2, 2).then_inc(psum_ready, 1)
            take(USE_LMOD)
            pe.wait_ge(acc_done, 4 * CPS + 4)
            column_sums(USE_LMOD, 0, accA)
            column_sums(USE_LMOD, 1, accB).then_inc(psum_ready, 1)
            for n in range(3):
                product(B_LAT, 0, 0, 2 * n, 2, USE_LAT + n, 0, lat, 0, lambda j: (op_lo, R_CQ + j + 1))
            for n in range(4):
                product(B_LAT, 0, 0, U_UQ + n, 1, USE_LAT + 3 + n, 0, lat, 4, lambda j: (op_lo, R_CKV + 1))
            pe.wait_ge(ld_const, 16)
            take(USE_ROT)
            rotate = consts[:, K_ROT:K_ROT + P]
            for b in range(2):
                pe.matmul(ps[USE_ROT % 2][:, b, :], rotate, rope_raw[:, 2 * b:2 * b + 2, :], start=True, stop=True)
            pe.matmul(ps[USE_ROT % 2][:, 2, 0:S], rotate, pT[:, T_KR, :], start=True, stop=True)\
                .then_inc(psum_ready, 1)
            pe.wait_ge(psum_free, USE_LAT + 7)
            for t in range(2):
                for k in range(H):
                    ins = pe.transpose(ps[USE_VM % 2][:, 2 * t + k // 4, (k % 4) * P:(k % 4 + 1) * P],
                                       vT[:, k, t * P:(t + 1) * P], ident)
            ins.then_inc(psum_ready, 1)
            take(USE_VS)
            for g, t0 in ((0, T_SB + 8), (1, T_FX + 8)):
                for t in range(2):
                    for k in range(4):
                        ins = pe.transpose(ps[USE_VS % 2][:, 2 * g + t, k * P:(k + 1) * P],
                                           pT[:, t0 + k, t * P:(t + 1) * P], ident)
            ins.then_inc(psum_ready, 1)

            def scores(i):
                s = ps[0][:, i % 2, :]
                n, tile, r = i % H, i % H // 2, DH * (i % 2)
                if i < ML0:
                    t0 = (T_SB if i < FX0 else T_FX) + tile
                    terms = [(pT[r:r + DH, t0, :], pT[r:r + DH, t0 + 4, :])]
                    if i >= FX0:
                        terms.append((foxA[:, :], foxB[:, n % 2, :]))
                else:
                    terms = [(q_nope[:, n, :], k_nope[:, n, :]),
                             (q_rope[r:r + DH, tile, :], pT[r:r + DH, T_KR, :])]
                if i >= 2:
                    pe.wait_ge(a_zm, i - 1)
                if FX0 <= i < ML0:
                    pe.wait_ge(fb_s, n + 1)
                for q in range(2):
                    for m, (lhs, rhs) in enumerate(terms):
                        ins = pe.matmul(s[:, q * P:(2 * q + 1) * P],
                                        lhs[:, q * P:(q + 1) * P], rhs[:, 0:(q + 1) * P],
                                        start=(m == 0), stop=(m == len(terms) - 1))
                ins.then_inc(a_sc, 1)

            def transpose_p(i):
                pe.wait_ge(a_p, i + 1)
                if i >= 2:
                    pe.wait_ge(a_pt, i - 1)
                for b in range(3):
                    ins = pe.transpose(ps[0][:, 2 + i % 2, b * P:(b + 1) * P], probs[i % 2][:, b * P:(b + 1) * P],
                                       ident)
                ins.then_inc(a_tr, 1)

            def weigh_v(i):
                d, n = (VD if i >= ML0 else DH), i % H
                v = (v_mla if i >= ML0 else v_fx if i >= FX0 else v_sb)[:, :, n * d:(n + 1) * d]
                pe.wait_ge(a_pt, i + 1)
                if i >= 2:
                    pe.wait_ge(a_o, i - 1)
                o, pt = ps[1][:, i % 2, :], probsT[i % 2]
                pe.matmul(o[:, 0:d], pt[:, 0:P], v[:, 0, :], start=True, stop=True)
                pe.matmul(o[:, d:2 * d], pt[:, P:2 * P], v[:, 0, :], start=True, stop=False)
                pe.matmul(o[:, d:2 * d], pt[:, 2 * P:3 * P], v[:, 1, :], start=False, stop=True).then_inc(a_pv, 1)

            pe.wait_ge(psum_free, USE_VS + 1)
            pe.wait_ge(q_sc, 2)
            pe.wait_ge(rope_c, 2)
            pe.wait_ge(fg_s, 1)
            pe.wait_ge(fm_s, 4)
            for t in range(HEADS + 4):
                if t < HEADS:
                    scores(t)
                if 0 <= t - 3 < HEADS:
                    transpose_p(t - 3)
                if 0 <= t - 4 < HEADS:
                    weigh_v(t - 4)
            for k in range(KT):
                use = USE_OT + k // 8
                pe.wait_ge(a_n, 2 + 2 * (k // 8))
                for q in range(2):
                    c = (k % 2) * S + q * P
                    ins = pe.transpose(ps[use % 2][:, k % 8 // 2, c:c + P], o_tok[q][:, k * P:(k + 1) * P], ident)
                if k % 8 == 7:
                    ins.then_inc(psum_ready, 1)
            with pe.Fori(0, 2) as it:
                for b in range(2):
                    product(B_OUT, 16, it, 8 * b, 8, USE_OUT + b, 2, hT, 0, lambda j: (op_lo, R_O + j + 1))
            take(USE_FSTAT)
            pe.wait_ge(ssq_done, 8)
            token_sums(USE_FSTAT, 0, ssq, 4).then_inc(psum_ready, 1)
            take(USE_FMOD)
            pe.wait_ge(acc_done, 5 * CPS + 5)
            column_sums(USE_FMOD, 0, accA).then_inc(psum_ready, 1)
            for half in range(2):
                base = B_FF + half * (U_FF1 + U_FF2)
                use1, use2 = ((USE_FF1A, USE_FF2A), (USE_FF1B, USE_FF2B))[half]
                with pe.Fori(0, 4) as it:
                    for b in range(2):
                        product(base, 16, it, 8 * b, 8, use1 + b, 2, hT, 0, lambda j: (op_lo, R_FFN + j + 1))
                if half == 0:
                    take(USE_GM)
                    pe.wait_ge(acc_done, 6 * CPS + 6)
                    column_sums(USE_GM, 0, accA).then_inc(psum_ready, 1)
                with pe.Fori(0, 2) as it:
                    for b in range(2):
                        product(base + U_FF1, 32, it, 16 * b, 16, use2 + b, 2, act, 0,
                                lambda j: (act_lo, 8 * half + j // 2 + 1))
            take(USE_END)
            pe.wait_ge(ssq_done, 12)
            token_sums(USE_END, 0, ssq, 4).then_inc(psum_ready, 1)


def feature_columns(v):
    return np.asarray(v).reshape(-1, P).T


def shape_constants():
    c = np.zeros((P, K_END), np.float32)
    c[:, K_ID:K_ID + P] = np.eye(P, dtype=np.float32)
    m = np.arange(P)
    low = m % ROPE < ROPE // 2
    c[m[low] + ROPE // 2, K_ROT + m[low]] = -1.0
    c[m[~low] - ROPE // 2, K_ROT + m[~low]] = 1.0
    inv = np.float32(ROPE_BASE) ** (-np.arange(0, ROPE, 2, dtype=np.float32) / np.float32(ROPE))
    ang = np.arange(S, dtype=np.float32)[None, :] * inv[m % (ROPE // 2)][:, None]
    c[:, K_COS:K_COS + S] = np.cos(ang)
    c[:, K_SIN:K_SIN + S] = np.sin(ang)
    q, k = m[:, None], m[None, :]
    for at, allowed in ((K_FOX, k <= q), (K_SB, k < q), (K_MLA, k < (q // CHUNK + 1) * CHUNK)):
        diagonal = np.where(allowed, 0.0, MASKED)
        c[:, at:at + P] = diagonal
        c[:, at + 2 * P:at + 3 * P] = diagonal
    c[:, K_SEG:K_SEG + 3 * P] = 1.0
    c[:, [K_SEG + P - 1, K_SEG + 3 * P - 1]] = 0.0
    for n in range(H):
        c[[n, 32 + n], K_SEL + n] = 1.0
    return c


def units_of(w):
    k, n = w.shape
    return w.reshape(k // (UK * P), UK, P, n // BW, BW).transpose(3, 0, 2, 1, 4).reshape(-1, P, UC)


def kernel(x, c, w_ada, b_ada, norm_mix, w_in, q_norm, w_uq, kv_norm, w_ukv, b_forget,
           out_norm, w_out, norm_ffn, w_ff1, w_ff2, final_norm):
    import concourse.bacc as bacc
    from concourse.bass_utils import run_bass_kernel_spmd

    f32 = np.float32
    a = lambda v: np.asarray(v)
    w_in, w_uq, w_ukv, w_ff1, w_ff2 = (a(w)[0] for w in (w_in, w_uq, w_ukv, w_ff1, w_ff2))
    lat = QL + KVL
    rope, gates = w_in[:, lat:lat + ROPE], w_in[:, -H:]
    pad = np.zeros((D, P - H), f32)
    w_in = np.concatenate([w_in[:, :lat], rope, rope, gates, pad, w_in[:, lat + ROPE:-H]], axis=1)
    uq = w_uq.reshape(QL, H, NOPE + ROPE)
    ukv = w_ukv.reshape(KVL, H, NOPE + VD)
    parts = [w_in,
             uq[:, :, :NOPE].reshape(QL, -1), uq[:, :, NOPE:].reshape(QL, -1),
             ukv[:, :, :NOPE].reshape(KVL, -1), ukv[:, :, NOPE:].reshape(KVL, -1), a(w_out)[0]]
    for h in range(2):
        parts += [w_ff1[:, h * FF // 2:(h + 1) * FF // 2], w_ff2[h * FF // 2:(h + 1) * FF // 2]]
    weights = np.concatenate([units_of(w) for w in parts])
    ada = a(w_ada)[0].reshape(KT, P, 6, D // AC, AC).transpose(2, 0, 3, 1, 4)
    ada = np.concatenate([ada[s] for s in SLICES]).reshape(-1, P, AC)
    cols = np.zeros((P, C_END), f32)
    for at, v in ((C_C, c), (C_B, a(b_ada)[0]), (C_MIX, a(norm_mix)[0]), (C_FFN, a(norm_ffn)[0]),
                  (C_OUT, a(out_norm)[0]), (C_FIN, final_norm), (C_QN, a(q_norm)[0]), (C_KVN, a(kv_norm)[0])):
        v = feature_columns(v)
        cols[:, at:at + v.shape[1]] = v
    cols[:H, C_BF] = a(b_forget)[0]
    cols[:, C_ONE:] = 1.0
    xt = a(x)[0].reshape(S, KT, P).transpose(2, 1, 0).reshape(P, -1)
    arrays = {"xt": xt, "cols": cols, "consts": shape_constants(), "ada": ada, "weights": weights}
    arrays = {n: np.ascontiguousarray(v) for n, v in arrays.items()}

    nc = bacc.Bacc("TRN2", target_bir_lowering=False, num_devices=1)
    aps = [nc.dram_tensor(f"in_{n}", v.shape, F32, kind="ExternalInput").ap() for n, v in arrays.items()]
    y = nc.dram_tensor("y", (P, KT * S), F32, kind="ExternalOutput").ap()
    hybrid_block(nc, *aps, y)
    r = run_bass_kernel_spmd(nc, [{f"in_{n}": v for n, v in arrays.items()}], core_ids=[0])
    got = r.results[0]["y"]
    return np.ascontiguousarray(got.reshape(P, KT, S).transpose(2, 1, 0).reshape(1, S, D))
```

```python
from contextlib import ExitStack

import numpy as np
import concourse.bass as bass
from concourse import mybir

P = 128
D, S, FF = 2048, 256, 8192
EPS = 1e-6
KT = D // P
H, QL, KVL, NOPE, ROPE, VD = 8, 512, 256, 128, 64, 128
DH = 64
CHUNK, ROPE_BASE = 64, 10000.0
MASKED = -1e30
BW = 512
UK = 2
UC = UK * BW
RING = 4
LAG = RING
AHEAD = LAG + RING

U_IN = 8 * (KT // UK)
U_UQ, U_UKV = 3 * (QL // P // UK), 4 * (KVL // P // UK)
U_LAT = U_UQ + U_UKV
LAT_ENDS = [1, 3, 5, 6, 7, 8, 9]
U_OUT = (D // BW) * (KT // UK)
HALF = FF // 2 // P
U_FF1 = (FF // 2 // BW) * (KT // UK)
U_FF2 = (D // BW) * (HALF // UK)
B_LAT = U_IN
B_OUT = B_LAT + U_LAT
B_FF = B_OUT + U_OUT
UNITS = B_FF + 2 * (U_FF1 + U_FF2)

AC = 1024
CPS = KT * (D // AC)
ADA = 4
SH_A, SC_A, G_A, SH_M, SC_M, G_M = range(6)
QT = KT // 4
QC = KT
A_GA, A_SHM, A_SCM, A_GM = (4 * QC + n * CPS for n in range(4))
Z_Q, Z_GA, Z_SHM, Z_SCM, Z_GM = (lambda q: q + 1), 5, 6, 7, 8

def use_in(q, blk):
    return 9 * q + 1 + blk


USE_LSTAT = 36
USE_LAT = 37
USE_ROT, USE_VM, USE_VS, USE_GA = 44, 45, 46, 47
USE_OT = 48
USE_SHM = 50
USE_OUT = 51
USE_FFN = 55
USE_FF1A, USE_GM, USE_FF2A = 56, 64, 65
USE_FF1B, USE_FF2B, USE_END = 69, 77, 81
READY = {use: n + 1 for n, use in enumerate((
    0, 9, 18, 27, USE_LSTAT, USE_ROT, USE_VM, USE_VS, USE_GA, USE_OT, USE_OT + 1, USE_SHM,
    USE_FFN, "ffn norm", USE_GM, USE_END))}
E_LAT, E_FF1A, E_FF1B = 32, 39, 47

R_MIX, R_CQ, R_CKV, R_O, R_FFN = 0, 8, 10, 11, 19

C_C, C_B, C_MIX, C_FFN, C_OUT, C_FIN, C_QN, C_KVN, C_BF, C_ONE = np.cumsum(
    [0, KT, 6 * KT, KT, KT, KT, KT, QL // P, KVL // P, 1]).tolist()
C_END = C_ONE + P
K_ID, K_ROT, K_COS, K_SIN, K_FOX, K_SB, K_MLA, K_SEG, K_SEL = np.cumsum(
    [0, P, P, S, S, 3 * P, 3 * P, 3 * P, 3 * P]).tolist()
K_END = K_SEL + H

F32, F32R = mybir.dt.float32, mybir.dt.float32r
ALU, ACT, AX = mybir.AluOpType, mybir.ActivationFunctionType, mybir.AxisListType

SB, ML, FX, HEADS = 0, 1, 2, 3 * H


def kind(i):
    return i % 3


def place(i):
    return (0, 2, 1)[kind(i)] * H + i // 3


def width(i):
    return VD if kind(i) == ML else DH


def softmaxes(i):
    return i - (i + 2) // 3


SCORE, MASK, SOFT, STICK, WEIGH, TURN, COPY, MIX, READ, SUM = range(10)
STEPS = HEADS + SUM
ZM = WEIGH - MASK + 1

T_CQ, T_CKV, T_KR, T_F, T_SB, T_FX = 0, 4, 6, 7, 8, 20


def hybrid_block(nc, xt_in, cols_in, consts_in, w_ada, weights, out):
    ctx = ExitStack()
    with ctx:
        def sb(name, shape, dt=F32, at=ctx):
            return at.enter_context(nc.sbuf_tensor(name, shape, dt))

        def sem(name):
            return ctx.enter_context(nc.semaphore(name))

        raw = sb("raw", [P, RING, UK, BW])
        w_hi = sb("w_hi", [P, RING, UK, BW], F32R)
        w_lo = sb("w_lo", [P, RING, UK, BW], F32R)
        xT = sb("xT", [P, KT, S])
        ada = sb("ada", [P, ADA, AC])
        accA = sb("accA", [P, D])
        tmp = sb("tmp", [P, 4, S])
        tmp2 = sb("tmp2", [P, 4, S])
        cols = sb("cols", [P, C_END])
        mod = sb("mod", [P, 6, KT])
        c_act = sb("c_act", [P, KT])
        gain = sb("gain", [P, KT])
        rstd = sb("rstd", [P, 2, S])
        small = sb("small", [P, 4 * KT])
        row = sb("row", [P, HEADS, 2])
        rinv = sb("rinv", [P, HEADS, 2])
        hss = sb("hss", [P, HEADS, 2])
        mx = sb("mx", [P, HEADS, 2])
        with ExitStack() as r:
            q_nope = sb("q_nope", [P, H, S], F32, r)
            k_nope = sb("k_nope", [P, H, S], F32, r)
            q_rope = sb("q_rope", [P, H // 2, S], F32, r)
            rope_raw = sb("rope_raw", [P, H // 2, S], F32, r)
            with ExitStack() as v:
                vT = sb("vT", [P, H, S], F32, v)
            o_tok0 = sb("o_tok0", [P, D], F32, r)
        hT = sb("hT", [P, KT, 2, S], F32R)
        with ExitStack() as r:
            foxA = sb("foxA", [P, S], F32, r)
            foxG = sb("foxG", [P, S], F32, r)
            foxB = sb("foxB", [P, 2, S], F32, r)
            pT = sb("pT", [P, 32, S], F32, r)
            consts = sb("consts", [P, K_END], F32, r)
            v_mla = sb("v_mla", [P, 2, H * VD], F32, r)
            o_tok1 = sb("o_tok1", [P, D], F32, r)
            with ExitStack() as v:
                lat = sb("lat", [P, 6, 2, S], F32R, v)
            zm = sb("zm", [P, ZM, 3 * P], F32, r)
            el = sb("el", [P, 2, 3 * P], F32, r)
            stick = sb("stick", [P, 2, 3 * P], F32, r)
        act = sb("act", [P, HALF, 2, S], F32R)
        ssq = sb("ssq", [P, 4, S])
        sq = sb("sq", [P, 4, S])
        v_sb = pT[:, T_CQ:T_CQ + 4, :].rearrange("p a b -> p (a b)").rearrange("p (t n) -> p t n", t=2)
        v_fx = pT[:, T_SB + 8:T_SB + 12, :].rearrange("p a b -> p (a b)").rearrange("p (t n) -> p t n", t=2)
        o_tok = [o_tok0, o_tok1]
        ones = cols[:, C_ONE:C_ONE + P]
        ident = consts[:, K_ID:K_ID + P]

        def scratch(t):
            return t[:, :, :].rearrange("p a b -> p (a b)")

        probs = [scratch(tmp)[:, i * 384:i * 384 + 384] for i in range(2)]
        probsT = [scratch(tmp2)[:, i * 384:i * 384 + 384] for i in range(2)]
        osq = [scratch(t)[:, 768:1024] for t in (tmp, tmp2)]
        neg_max = small[:, 0:2]

        ps = [ctx.enter_context(nc.psum_tensor(f"ps{i}", [P, 4, 512], F32)) for i in range(2)]

        ld_cols, ld_x, ld_const, ld_out = sem("ld_cols"), sem("ld_x"), sem("ld_const"), sem("ld_out")
        raw_full = [sem(f"raw_full{i}") for i in range(RING)]
        ada_full = [sem(f"ada_full{i}") for i in range(ADA)]
        hi_done = sem("hi_done")
        lo_vec, lo_pool = sem("lo_vec"), sem("lo_pool")
        unit_used = sem("unit_used")
        psum_ready = sem("psum_ready")
        psum_free = sem("psum_free")
        tmp_ready = sem("tmp_ready")
        acc_done = sem("acc_done")
        silu_s, mod_s, gain_s = sem("silu_s"), sem("mod_s"), sem("gain_s")
        x_half = sem("x_half")
        zeroed = sem("zeroed")
        part_added = sem("part_added")
        x_new = sem("x_new")
        sq_done, ssq_done = sem("sq_done"), sem("ssq_done")
        ms_s, rt_s, rstd_s = sem("ms_s"), sem("rt_s"), sem("rstd_s")
        t_ready, op_hi, op_lo = sem("t_ready"), sem("op_hi"), sem("op_lo")
        relu2, act_hi, act_lo = sem("relu2"), sem("act_hi"), sem("act_lo")
        lsq = sem("lsq")
        rope_s, rope_c = sem("rope_s"), sem("rope_c")
        va_s = sem("va_s")
        f_s, fa_s, fg_s, fb_s, fm_s = sem("f_s"), sem("fa_s"), sem("fg_s"), sem("fb_s"), sem("fm_s")
        a_sc, a_zm, a_mx, a_ab, a_ex, a_ln = (sem(n) for n in ("a_sc", "a_zm", "a_mx", "a_ab", "a_ex", "a_ln"))
        a_sp, a_scan, a_w, a_p, a_tr, a_pt, a_pv = (
            sem(n) for n in ("a_sp", "a_scan", "a_w", "a_p", "a_tr", "a_pt", "a_pv"))
        a_ri, a_o, a_sq, a_ss, a_n, a_np = (sem(n) for n in ("a_ri", "a_o", "a_sq", "a_ss", "a_n", "a_np"))
        q_sc, fin_s = sem("q_sc"), sem("fin_s")

        block = ctx.enter_context(nc.Block())

        def lo_count(u0, step, it, j):
            return (u0 + j) // 2 + 1 + (step // 2) * it

        def lo_sem(u):
            return lo_vec if u % 2 == 0 else lo_pool

        def scaled(n):
            return n - 8 if n >= R_FFN else n

        def head_col(i):
            return VD * (i // 3) if kind(i) == ML else H * VD + DH * place(i)

        @block.sync
        def _(sp):
            def load_unit(u0, step, it, j, fresh=False):
                if not fresh:
                    sp.wait_ge(lo_sem(u0 + j), lo_count(u0 - RING, step, it, j))
                slot = (u0 + j) % RING
                sp.dma_start(raw[:, slot, :, :].rearrange("p k n -> p (k n)"),
                             weights[u0 + j + step * it, :, :]).then_inc(raw_full[slot], 16)

            def load_ada(a0, zeros, step, it, j, fresh=False):
                if not fresh:
                    sp.wait_ge(acc_done, a0 + j - ADA + 1 + zeros + step * it)
                slot = (a0 + j) % ADA
                sp.dma_start(ada[:, slot, :], w_ada[a0 + j + step * it, :, :]).then_inc(ada_full[slot], 16)

            sp.dma_start(cols[:, :], cols_in).then_inc(ld_cols, 16)
            for j in range(ADA):
                load_ada(0, 0, 0, 0, j, fresh=True)
            sp.dma_start(xT[:, :, :].rearrange("p k t -> p (k t)"), xt_in).then_inc(ld_x, 16)
            for j in range(8):
                load_ada(ADA, Z_Q(0), 0, 0, j)
            for j in range(RING):
                load_unit(0, 0, 0, j, fresh=True)
            for j in range(4):
                load_ada(12, Z_Q(0), 0, 0, j)
            for j in range(4):
                load_ada(QC, Z_Q(0), 0, 0, j)
            for j in range(RING):
                load_unit(RING, 0, 0, j)
            for q in range(4):
                if q == 3:
                    sp.dma_start(consts[:, :], consts_in).then_inc(ld_const, 16)
                with sp.Fori(0, QC // 4) as it:
                    for j in range(RING):
                        load_unit(QC * q + AHEAD, RING, it, j)
                        load_ada(QC * (q + 1) + ADA, Z_Q(q + 1), ADA, it, j)
            loaded = AHEAD
            for n in range(8):
                if n < 7:
                    for u in range(loaded, LAT_ENDS[n] + 1 + AHEAD):
                        load_unit(B_LAT, 0, 0, u)
                    loaded = LAT_ENDS[n] + 1 + AHEAD
                for j in range(2):
                    load_ada(A_GA + QC + ADA + 2 * n, Z_GA, 0, 0, j)
            with sp.Fori(0, CPS // ADA) as it:
                for j in range(ADA):
                    load_ada(A_SHM + ADA, Z_SHM, ADA, it, j)
            with sp.Fori(0, U_OUT // RING) as it:
                for j in range(RING):
                    load_unit(B_OUT + AHEAD, RING, it, j)
                    load_ada(A_SCM + ADA, Z_SCM, RING, it, j)
            with sp.Fori(0, CPS // 4 - 1) as it:
                for j in range(8):
                    load_unit(B_FF + AHEAD, 8, it, j)
                    if j % 2 == 1:
                        load_ada(A_GM + ADA, Z_GM, ADA, it, j // 2)
            rest = B_FF + AHEAD + 2 * (CPS - ADA)
            with sp.Fori(0, (UNITS - rest) // RING) as it:
                for j in range(RING):
                    load_unit(rest, RING, it, j)
            for j in range(4):
                sp.wait_ge(fin_s, 4 * j + 4)
                src = (tmp, tmp2, sq, ssq)[j]
                sp.dma_start(out[:, 4 * j * S:(4 * j + 4) * S], scratch(src)).then_inc(ld_out, 16)
            sp.wait_ge(ld_out, 64)

        @block.scalar
        def _(sc):
            def hi(u0, step, it, j):
                slot = (u0 + j) % RING
                sc.wait_ge(raw_full[slot], 16 * ((u0 + j) // RING + 1) + (16 * step // RING) * it)
                if u0 + j >= RING:
                    sc.wait_ge(unit_used, u0 + j - RING + 1 + step * it)
                sc.activation(w_hi[:, slot, :, :], raw[:, slot, :, :], ACT.Copy).then_inc(hi_done, 1)

            def copy_low(use, used, step, it):
                sc.wait_ge(unit_used, used + step * it)
                sc.wait_ge(psum_free, use + 1 + 2 * it)
                sc.activation(tmp[:, :, :], ps[use % 2][:, :, S:2 * S], ACT.Copy).then_inc(tmp_ready, 1)

            def square(blocks, it, blk, added):
                sc.wait_ge(x_new, 4 * blocks + 8 * it)
                sc.wait_ge(ssq_done, added)
                sc.activation(sq[:, :, :], xT[:, bass.ds(blk, 4), :], ACT.Square).then_inc(sq_done, 1)

            def square_tiles(blocks, added):
                sc.wait_ge(ssq_done, added)
                for n in range(4):
                    sc.wait_ge(x_new, 4 * blocks - 3 + n)
                    sc.activation(sq[:, n, :], xT[:, KT - 4 + n, :], ACT.Square).then_inc(sq_done, 1)

            def root(n, halves=1):
                sc.wait_ge(ms_s, n)
                sc.activation(rstd[:, 0:halves, :], rstd[:, 0:halves, :], ACT.Sqrt).then_inc(rt_s, 1)

            def operand_hi(n, dst, bias):
                sc.wait_ge(t_ready, scaled(n) + 1)
                t = tmp[:, 2 * (n % 2):2 * (n % 2) + 2, :]
                if bias is None:
                    sc.activation(dst[:, :, 0, :], t, ACT.Copy).then_inc(op_hi, 1)
                else:
                    sc.activation(dst[:, 0, 0, :], t[:, 0, :], ACT.Identity, bias=bias[:, 0:1])
                    sc.activation(dst[:, 1, 0, :], t[:, 1, :], ACT.Identity, bias=bias[:, 1:2]).then_inc(op_hi, 1)

            sc.wait_ge(ld_cols, 16)
            sc.activation(c_act[:, :], cols[:, C_C:C_C + KT], ACT.Exp, scale=-1.0).then_inc(silu_s, 1)
            sc.wait_ge(ld_x, 16)
            for b in range(4):
                if b:
                    sc.wait_ge(ssq_done, b)
                sc.activation(sq[:, :, :], xT[:, 4 * b:4 * b + 4, :], ACT.Square).then_inc(sq_done, 1)
            for j in range(RING):
                hi(0, 0, 0, j)
            root(1)
            for q in range(4):
                sc.wait_ge(mod_s, 2 * q + 2)
                for j in range(2 * q, 2 * q + 2):
                    operand_hi(R_MIX + j, hT[:, 2 * j:2 * j + 2, :, :], mod[:, SH_A, 2 * j:2 * j + 2])
                with sc.Fori(0, 4) as it:
                    for b in range(2):
                        for j in range(2):
                            hi(QC * q + LAG, 4, it, 2 * b + j)
                        copy_low(use_in(q, b), QC * q + 2 * b + 2, 4, it)
            sc.wait_ge(part_added, 33)
            for i, n in ((0, 4), (1, 2)):
                if i:
                    sc.wait_ge(lsq, 1)
                sc.activation(tmp2[:, 0:n, :], pT[:, T_CQ + 4 * i:T_CQ + 4 * i + n, :],
                              ACT.Square).then_inc(sq_done, 1)
            root(2, halves=2)
            for n in range(3):
                operand_hi(R_CQ + n, lat[:, 2 * n:2 * n + 2, :, :], None)
            fx = foxB[0:H, 0, :]
            fl = foxB[0:H, 1, :]
            sc.wait_ge(f_s, 1)
            sc.activation(fl, fx, ACT.Abs).then_inc(f_s, 1)
            sc.wait_ge(f_s, 2)
            sc.activation(fl, fl, ACT.Exp, scale=-1.0).then_inc(f_s, 1)
            sc.wait_ge(f_s, 3)
            sc.activation(fl, fl, ACT.Ln, bias=cols[0:H, C_ONE:C_ONE + 1]).then_inc(f_s, 1)
            sc.wait_ge(f_s, 6)
            sc.activation(foxG[32:32 + H, :], foxA[0:H, :], ACT.Copy, scale=-1.0).then_inc(fg_s, 1)
            for n, e in enumerate(LAT_ENDS):
                for u in range(LAG if n == 0 else LAT_ENDS[n - 1] + 1 + LAG, e + 1 + LAG):
                    hi(B_LAT, 0, 0, u)
                copy_low(USE_LAT + n, B_LAT + e + 1, 0, 0)
            sc.wait_ge(psum_ready, READY[USE_VM])
            sc.activation(v_mla[:, 0, :], ps[USE_VM % 2][:, 0:2, :].rearrange("p a b -> p (a b)"),
                          ACT.Copy).then_inc(va_s, 1)
            sc.wait_ge(psum_ready, READY[USE_VS])
            sc.activation(v_sb, ps[USE_VS % 2][:, 0:2, :], ACT.Copy).then_inc(va_s, 1)

            def soft_parts(i):
                n = i // 3
                e = el[:, n % 2, :]
                sc.wait_ge(a_zm, i + 1)
                if n >= 2:
                    sc.wait_ge(a_scan, n - 1)
                sc.activation(e, zm[:, i % ZM, :], ACT.Abs).then_inc(a_ab, 1)
                sc.wait_ge(a_ab, n + 1)
                sc.activation(e, e, ACT.Exp, scale=-1.0).then_inc(a_ex, 1)
                sc.wait_ge(a_ex, n + 1)
                sc.activation(e, e, ACT.Ln, bias=cols[:, C_ONE:C_ONE + 1]).then_inc(a_ln, 1)

            def weights_of(i):
                p = probs[i % 2]
                if i >= 2:
                    sc.wait_ge(a_tr, i - 1)
                if kind(i) == SB:
                    sc.wait_ge(a_w, i // 3 + 1)
                    sc.activation(p, zm[:, i % ZM, :], ACT.Exp).then_inc(a_p, 1)
                else:
                    sc.wait_ge(a_mx, 2 * softmaxes(i) + 2)
                    sc.activation(p[:, 0:P], zm[:, i % ZM, 0:P], ACT.Exp, bias=mx[:, place(i), 0:1],
                                  accum_out=row[:, place(i), 0:1])
                    sc.activation(p[:, P:3 * P], zm[:, i % ZM, P:3 * P], ACT.Exp, bias=mx[:, place(i), 1:2],
                                  accum_out=row[:, place(i), 1:2]).then_inc(a_p, 1)

            def copy_pt(i):
                sc.wait_ge(a_tr, i + 1)
                if i >= 2:
                    sc.wait_ge(a_pv, i - 1)
                sc.activation(probsT[i % 2], ps[0][:, 2 + i % 2, 0:3 * P], ACT.Copy).then_inc(a_pt, 1)

            for t in range(STEPS):
                if 0 <= t - SOFT < HEADS and kind(t - SOFT) == SB:
                    soft_parts(t - SOFT)
                if 0 <= t - WEIGH < HEADS:
                    weights_of(t - WEIGH)
                if 0 <= t - COPY < HEADS:
                    copy_pt(t - COPY)
            sc.wait_ge(ms_s, 3)
            sc.activation(hss[:, :, :], hss[:, :, :], ACT.Sqrt).then_inc(rt_s, 1)
            for j in range(8):
                use = USE_OT + j // 4
                if j % 4 == 0:
                    sc.wait_ge(psum_ready, READY[use])
                for k in range(2):
                    c = C_OUT + 2 * j + k
                    ins = sc.activation(hT[:, 2 * j + k, 0, :], ps[use % 2][:, j % 4, k * S:(k + 1) * S],
                                        ACT.Copy, scale=cols[:, c:c + 1])
                ins.then_inc(op_hi, 1)
            for b in range(4):
                for j in range(8):
                    hi(B_OUT + LAG, 0, 0, 8 * b + j)
                if b < 3:
                    square(b + 1, 0, 4 * b, 4 + b)
            square_tiles(4, 7)
            root(4)
            for j in range(8):
                if j == 0:
                    sc.wait_ge(mod_s, 10)
                operand_hi(R_FFN + j, hT[:, 2 * j:2 * j + 2, :, :], mod[:, SH_M, 2 * j:2 * j + 2])

            for half in range(2):
                base = B_FF + half * (U_FF1 + U_FF2)
                use1 = (USE_FF1A, USE_FF1B)[half]
                with sc.Fori(0, 4) as it:
                    for b in range(2):
                        for j in range(8):
                            hi(base + LAG, 16, it, 8 * b + j)
                        copy_low(use1 + b, base + 8 * b + 8, 16, it)
                        sc.wait_ge(relu2, 8 * half + b + 1 + 2 * it)
                        sc.activation(act[:, bass.ds(4 * b + 8 * it, 4), 0, :], tmp2[:, :, :],
                                      ACT.Copy).then_inc(act_hi, 1)

                def down(it, last=False):
                    for b in range(2):
                        for j in range(16):
                            if not (last and b == 1 and j >= 16 - LAG):
                                hi(base + U_FF1 + LAG, 32, it, 16 * b + j)
                        if last and b == 1:
                            square_tiles(12, 10)
                        elif half == 1:
                            square(8 + b + 1, it, 4 * b + 8 * it, 7 + b + 2 * it)

                if half == 0:
                    with sc.Fori(0, 2) as it:
                        down(it)
                else:
                    down(0)
                    down(1, last=True)
            root(5)

        @block.gpsimd
        def _(gp):
            def lo(u0, step, it, j):
                if (u0 + j) % 2 == 1:
                    slot = (u0 + j) % RING
                    gp.wait_ge(hi_done, u0 + j + 1 + step * it)
                    gp.tensor_tensor(w_lo[:, slot, :, :], raw[:, slot, :, :],
                                     w_hi[:, slot, :, :].bitcast(F32), ALU.subtract).then_inc(lo_pool, 1)

            def add_squares(n):
                gp.wait_ge(sq_done, n)
                gp.tensor_tensor(ssq[:, :, :], ssq[:, :, :], sq[:, :, :], ALU.add).then_inc(ssq_done, 1)

            gp.memset(ssq[:, :, :], 0.0).then_inc(zeroed, 1)
            gp.memset(pT[:, :, :], 0.0).then_inc(part_added, 1)
            gp.wait_ge(zeroed, 1)
            for b in range(4):
                add_squares(b + 1)
            for j in range(RING):
                lo(0, 0, 0, j)
            for q in range(4):
                with gp.Fori(0, 4) as it:
                    for b in range(2):
                        for j in range(2):
                            lo(QC * q + LAG, 4, it, 2 * b + j)
                        gp.wait_ge(psum_free, use_in(q, b) + 2 + 2 * it)
                        gp.wait_ge(part_added, 8 * q + b + 1 + 2 * it)
                        part = pT[:, bass.ds(4 * b + 8 * it, 4), :]
                        gp.tensor_tensor(part, part, tmp2[:, :, :], ALU.add).then_inc(part_added, 1)
            gp.memset(foxA[:, :], 0.0).then_inc(fm_s, 1)
            gp.memset(foxG[:, :], 0.0).then_inc(fm_s, 1)
            gp.wait_ge(fm_s, 2)
            gp.memset(foxA[32:32 + H, :], 1.0).then_inc(fm_s, 1)
            gp.wait_ge(fm_s, 3)
            gp.memset(foxG[0:H, :], 1.0).then_inc(fm_s, 1)
            gp.wait_ge(fm_s, 4)
            for j in range(LAG, U_LAT + LAG):
                lo(B_LAT, 0, 0, j)

            def stick_weight(i):
                gp.wait_ge(a_scan, i // 3 + 1)
                z = zm[:, i % ZM, :]
                gp.tensor_tensor(z, z, stick[:, i // 3 % 2, :], ALU.subtract).then_inc(a_w, 1)

            def fox_operand(i):
                n = i // 3
                if n >= 2:
                    gp.wait_ge(a_sc, i - 5)
                gp.tensor_scalar(foxB[:, n % 2, :], foxG[:, :], consts[:, K_SEL + n:K_SEL + n + 1], None,
                                 ALU.mult).then_inc(fb_s, 1)

            def out_square(i):
                d = width(i)
                gp.wait_ge(a_o, i + 1)
                if i >= 2:
                    gp.wait_ge(a_ss, i - 1)
                for q in range(2):
                    o = o_tok[q][:, head_col(i):head_col(i) + d]
                    ins = gp.tensor_tensor(osq[i % 2][:, q * d:q * d + d], o, o, ALU.mult)
                ins.then_inc(a_sq, 1)

            gp.wait_ge(fg_s, 1)
            for t in range(STEPS):
                if t + 2 < HEADS and kind(t + 2) == FX:
                    fox_operand(t + 2)
                if 0 <= t - STICK < HEADS and kind(t - STICK) == SB:
                    stick_weight(t - STICK)
                if 0 <= t - READ < HEADS:
                    out_square(t - READ)
            gp.wait_ge(a_ri, 2 * H + 1)
            o = o_tok[1][:, H * VD:].rearrange("p (h d) -> p h d", d=DH)
            gp.tensor_tensor(o, o, hss[:, 0:2 * H, 1].unsqueeze(2).to_broadcast([P, 2 * H, DH]),
                             ALU.mult).then_inc(a_np, 1)
            gp.memset(ssq[:, :, :], 0.0).then_inc(zeroed, 1)
            gp.wait_ge(zeroed, 2)
            for b in range(4):
                for j in range(8):
                    lo(B_OUT + LAG, 0, 0, 8 * b + j)
                if b < 3:
                    add_squares(6 + b + 1)
            gp.wait_ge(psum_ready, READY["ffn norm"])
            gp.memset(ssq[:, :, :], 0.0).then_inc(zeroed, 1)
            gp.wait_ge(zeroed, 3)
            for half in range(2):
                base = B_FF + half * (U_FF1 + U_FF2)
                with gp.Fori(0, 4) as it:
                    for j in range(16):
                        lo(base + LAG, 16, it, j)

                def down(it, last=False):
                    for b in range(2):
                        for j in range(16):
                            if not (last and b == 1 and j >= 16 - LAG):
                                lo(base + U_FF1 + LAG, 32, it, 16 * b + j)
                        if half == 1 and not (last and b == 1):
                            add_squares(13 + b + 1 + 2 * it)

                if half == 0:
                    with gp.Fori(0, 2) as it:
                        down(it)
                else:
                    down(0)
                    down(1, last=True)

        @block.vector
        def _(ve):
            def lo(u0, step, it, j):
                if (u0 + j) % 2 == 0:
                    slot = (u0 + j) % RING
                    ve.wait_ge(hi_done, u0 + j + 1 + step * it)
                    ve.tensor_tensor(w_lo[:, slot, :, :], raw[:, slot, :, :],
                                     w_hi[:, slot, :, :].bitcast(F32), ALU.subtract).then_inc(lo_vec, 1)

            def add_chunk(a0, kt0, zeros, step, it, j):
                slot = (a0 + j) % ADA
                early = a0 < A_GA
                half = (a0 // QC) % 2 if early else (a0 + j) % 2
                kt = kt0 + j + step * it if early else kt0 + j // 2 + (step // 2) * it
                ve.wait_ge(ada_full[slot], 16 * ((a0 + j) // ADA + 1) + (16 * step // ADA) * it)
                ve.wait_ge(acc_done, a0 + j - (0 if early else 1) + zeros + step * it)
                dst = accA[:, half * AC:(half + 1) * AC]
                ve.scalar_tensor_tensor(out=dst, in0=ada[:, slot, :], scalar=c_act[:, bass.ds(kt, 1)],
                                        in1=dst, op0=ALU.mult, op1=ALU.add).then_inc(acc_done, 1)

            def clear_acc(halves, chunks, zeros):
                lo_h, hi_h = halves
                ve.memset(accA[:, lo_h * AC:hi_h * AC], 0.0).then_inc(acc_done, 1)
                ve.wait_ge(acc_done, chunks + zeros)

            def mean(use, bank, half, width):
                return ve.tensor_scalar(rstd[:, half, :], ps[use % 2][:, bank, 0:S], 1.0 / width, EPS,
                                        ALU.mult, ALU.add)

            def invert(n, done, halves=1):
                ve.wait_ge(rt_s, n)
                ve.reciprocal(rstd[:, 0:halves, :], rstd[:, 0:halves, :]).then_inc(rstd_s, 1)
                ve.wait_ge(rstd_s, done)

            def read_mod(use, bank, g, k0=0, n=KT, at=0):
                src = C_B + KT * g + k0
                return ve.tensor_tensor(mod[:, g, k0:k0 + n], ps[use % 2][:, bank, at:at + n],
                                        cols[:, src:src + n], ALU.add)

            def make_gain(g, c, k0=0, n=KT):
                ve.scalar_tensor_tensor(out=gain[:, k0:k0 + n], in0=mod[:, g, k0:k0 + n], scalar=1.0,
                                        in1=cols[:, c + k0:c + k0 + n], op0=ALU.add,
                                        op1=ALU.mult).then_inc(gain_s, 1)

            def slot_of(n):
                return tmp[:, 2 * (n % 2):2 * (n % 2) + 2, :]

            def scaled_pair(n, src, g, half):
                if n >= 2:
                    ve.wait_ge(op_lo, n - 1)
                for k in range(2):
                    ins = ve.scalar_tensor_tensor(out=slot_of(n)[:, k, :], in0=src[:, k, :], scalar=g[:, k:k + 1],
                                                  in1=rstd[:, half, :], op0=ALU.mult, op1=ALU.mult)
                ins.then_inc(t_ready, 1)

            def operand_lo(n, dst, bias):
                ve.wait_ge(op_hi, n + 1)
                if bias is None:
                    ve.tensor_tensor(dst[:, :, 1, :], slot_of(n), dst[:, :, 0, :].bitcast(F32),
                                     ALU.subtract).then_inc(op_lo, 1)
                else:
                    for k in range(2):
                        ins = ve.scalar_tensor_tensor(out=dst[:, k, 1, :], in0=slot_of(n)[:, k, :],
                                                      scalar=bias[:, k:k + 1], in1=dst[:, k, 0, :].bitcast(F32),
                                                      op0=ALU.add, op1=ALU.subtract)
                    ins.then_inc(op_lo, 1)

            def modulated_norm(r0, shift, j0, j1):
                for j in range(j0, j1 + 1):
                    if j < j1:
                        scaled_pair(r0 + j, xT[:, 2 * j:2 * j + 2, :], gain[:, 2 * j:2 * j + 2], 0)
                    if j > j0:
                        i = j - 1
                        operand_lo(r0 + i, hT[:, 2 * i:2 * i + 2, :, :], mod[:, shift, 2 * i:2 * i + 2])

            def sum_halves(dst, use, n_use, e, n_e, it, done):
                ve.wait_ge(tmp_ready, e + 1 + n_e * it)
                ve.tensor_tensor(dst, ps[use % 2][:, :, 0:S], tmp[:, :, :], ALU.add).then_inc(done, 1)

            def gate_block(use, used, step, blocks, blk, g, it):
                ve.wait_ge(unit_used, used + step * it)
                for half, done in ((1, x_half), (0, x_new)):
                    for n in range(4):
                        if half == 0:
                            ve.wait_ge(x_half, 4 * blocks + n + 1 + 8 * it)
                        x = xT[:, bass.ds(blk + n, 1), :].rearrange("p k t -> p (k t)")
                        ve.scalar_tensor_tensor(out=x, in0=ps[use % 2][:, n, half * S:(half + 1) * S],
                                                scalar=mod[:, g, bass.ds(blk + n, 1)], in1=x,
                                                op0=ALU.mult, op1=ALU.add).then_inc(done, 1)
                ve.wait_ge(x_new, 4 * blocks + 4 + 8 * it)
                ve.sem_inc(psum_free, 1)

            ve.sem_inc(psum_free, 1)
            clear_acc((0, 1), 0, 1)
            ve.wait_ge(silu_s, 1)
            den = small[:, 0:KT]
            ve.tensor_scalar(den, c_act[:, :], 1.0, None, ALU.add).then_inc(silu_s, 1)
            ve.wait_ge(silu_s, 2)
            ve.reciprocal(den, den).then_inc(silu_s, 1)
            ve.wait_ge(silu_s, 3)
            ve.tensor_tensor(c_act[:, :], cols[:, C_C:C_C + KT], den, ALU.mult).then_inc(silu_s, 1)
            ve.wait_ge(silu_s, 4)
            with ve.Fori(0, QC // 4) as it:
                for j in range(4):
                    add_chunk(0, 0, Z_Q(0), 4, it, j)
            for j in range(RING):
                lo(0, 0, 0, j)
            for q in range(4):
                use = 9 * q
                ve.wait_ge(psum_ready, READY[use])
                if q == 0:
                    mean(use, 1, 0, D).then_inc(ms_s, 1)
                read_mod(use, 0, SC_A, QT * q, QT, 0).then_inc(mod_s, 1)
                read_mod(use, 0, SH_A, QT * q, QT, QT).then_inc(mod_s, 1)
                ve.wait_ge(mod_s, 2 * q + 2)
                if q == 0:
                    ve.wait_ge(ms_s, 1)
                ve.sem_inc(psum_free, 1)
                make_gain(SC_A, C_MIX, QT * q, QT)
                ve.wait_ge(gain_s, q + 1)
                if q == 0:
                    invert(1, 1)
                modulated_norm(R_MIX, SH_A, 2 * q, 2 * q + 2)
                halves = ((q + 1) % 2, (q + 1) % 2 + 1) if q < 3 else (0, 2)
                clear_acc(halves, QC * (q + 1), Z_Q(q + 1))
                with ve.Fori(0, 4) as it:
                    for b in range(2):
                        for j in range(2 * b, 2 * b + 2):
                            lo(QC * q + LAG, 4, it, j)
                            add_chunk(QC * (q + 1), 0, Z_Q(q + 1), 4, it, j)
                        ve.wait_ge(part_added, 8 * q + b + 1 + 2 * it)
                        sum_halves(tmp2[:, :, :], use_in(q, b), 2, 8 * q + b, 2, it, psum_free)
            ve.wait_ge(psum_ready, READY[USE_LSTAT])
            ve.wait_ge(part_added, 33)
            mean(USE_LSTAT, 0, 0, QL)
            mean(USE_LSTAT, 1, 1, KVL).then_inc(ms_s, 1)
            ve.wait_ge(ms_s, 2)
            ve.sem_inc(psum_free, 1)
            invert(2, 2, halves=2)
            for n in range(4):
                if n < 3:
                    g = C_QN + 2 * n
                    scaled_pair(R_CQ + n, pT[:, T_CQ + 2 * n:T_CQ + 2 * n + 2, :], cols[:, g:g + 2], n // 2)
                if n:
                    operand_lo(R_CQ + n - 1, lat[:, 2 * n - 2:2 * n, :, :], None)
            fx, fl = foxB[0:H, 0, :], foxB[0:H, 1, :]
            ve.tensor_scalar(fx, pT[0:H, T_F, :], cols[0:H, C_BF:C_BF + 1], None, ALU.add).then_inc(f_s, 1)
            ve.tensor_scalar(pT[:, T_SB:T_SB + 4, :], pT[:, T_SB:T_SB + 4, :], DH ** -0.5, None,
                             ALU.mult).then_inc(q_sc, 1)
            ve.tensor_scalar(pT[:, T_FX:T_FX + 4, :], pT[:, T_FX:T_FX + 4, :], DH ** -0.5, None,
                             ALU.mult).then_inc(q_sc, 1)
            ve.wait_ge(f_s, 4)
            ve.scalar_tensor_tensor(out=fx, in0=fx, scalar=0.0, in1=fl, op0=ALU.min,
                                    op1=ALU.subtract).then_inc(f_s, 1)
            ve.wait_ge(f_s, 5)
            ve.wait_ge(fm_s, 2)
            ve.tensor_tensor_scan(foxA[0:H, :], consts[0:H, K_SEG:K_SEG + 1].to_broadcast([H, S]), fx, 0.0, ALU.mult, ALU.add).then_inc(f_s, 1)
            dests = [q_nope[:, 0:4, :], q_nope[:, 4:8, :], rope_raw[:, :, :], k_nope[:, 0:4, :],
                     k_nope[:, 4:8, :], vT[:, 0:4, :], vT[:, 4:8, :]]
            for n, e in enumerate(LAT_ENDS):
                for u in range(LAG if n == 0 else LAT_ENDS[n - 1] + 1 + LAG, e + 1 + LAG):
                    lo(B_LAT, 0, 0, u)
                for j in range(QC + 2 * n, QC + 2 * n + 2):
                    add_chunk(A_GA, 0, Z_GA, 0, 0, j)
                sum_halves(dests[n], USE_LAT + n, 0, E_LAT + n, 0, 0, psum_free)
            for j in range(QC + 14, CPS):
                add_chunk(A_GA, 0, Z_GA, 0, 0, j)
            cos, sin = consts[:, K_COS:K_COS + S], consts[:, K_SIN:K_SIN + S]
            cos4 = cos.unsqueeze(1).to_broadcast([P, 4, S])
            sin4 = sin.unsqueeze(1).to_broadcast([P, 4, S])
            rot = ps[USE_ROT % 2]
            ve.tensor_tensor(q_rope[:, :, :], rope_raw[:, :, :], cos4, ALU.mult).then_inc(rope_s, 1)
            ve.tensor_tensor(rstd[:, 0, :], pT[:, T_KR, :], cos, ALU.mult).then_inc(rope_s, 1)
            ve.wait_ge(psum_ready, READY[USE_ROT])
            ve.tensor_tensor(tmp2[:, :, :], rot[:, 0:2, :].rearrange("p b (h t) -> p (b h) t", h=2), sin4,
                             ALU.mult).then_inc(rope_s, 1)
            ve.tensor_tensor(rstd[:, 1, :], rot[:, 2, 0:S], sin, ALU.mult).then_inc(rope_s, 1)
            ve.wait_ge(rope_s, 4)
            ve.sem_inc(psum_free, 1)
            ve.tensor_tensor(q_rope[:, :, :], q_rope[:, :, :], tmp2[:, :, :], ALU.add).then_inc(rope_c, 1)
            ve.tensor_tensor(pT[:, T_KR, :], rstd[:, 0, :], rstd[:, 1, :], ALU.add).then_inc(rope_c, 1)
            ve.wait_ge(va_s, 1)
            ve.tensor_copy(v_mla[:, 1, :], ps[USE_VM % 2][:, 2:4, :].rearrange("p a b -> p (a b)"))\
                .then_inc(psum_free, 1)
            ve.wait_ge(va_s, 2)
            ve.tensor_copy(v_fx, ps[USE_VS % 2][:, 2:4, :]).then_inc(psum_free, 1)
            ve.wait_ge(psum_ready, READY[USE_GA])
            read_mod(USE_GA, 0, G_A).then_inc(mod_s, 1)
            ve.wait_ge(mod_s, 9)
            ve.sem_inc(psum_free, 1)
            clear_acc((0, 2), A_SHM, Z_SHM)

            def masked_scores(i):
                s = ps[0][:, i % 2, 0:3 * P]
                z = zm[:, i % ZM, :]
                ve.wait_ge(a_sc, i + 1)
                if i >= ZM:
                    ve.wait_ge(a_p, i - ZM + 1)
                if kind(i) == ML:
                    ve.scalar_tensor_tensor(out=z, in0=s, scalar=(NOPE + ROPE) ** -0.5,
                                            in1=consts[:, K_MLA:K_MLA + 3 * P], op0=ALU.mult,
                                            op1=ALU.add).then_inc(a_zm, 1)
                else:
                    k = K_SB if kind(i) == SB else K_FOX
                    ve.tensor_tensor(z, s, consts[:, k:k + 3 * P], ALU.add).then_inc(a_zm, 1)
                if kind(i) != SB:
                    ve.wait_ge(a_zm, i + 1)
                    ve.tensor_reduce(mx[:, place(i), 0:1], z[:, 0:P], AX.X, ALU.max, negate=True).then_inc(a_mx, 1)
                    ve.tensor_reduce(mx[:, place(i), 1:2], z[:, P:3 * P], AX.X, ALU.max, negate=True).then_inc(a_mx, 1)

            def stick_sums(i):
                n = i // 3
                e, z, r = el[:, n % 2, :], zm[:, i % ZM, :], stick[:, n % 2, :]
                ve.wait_ge(a_ln, n + 1)
                ve.scalar_tensor_tensor(out=e, in0=z, scalar=0.0, in1=e, op0=ALU.max,
                                        op1=ALU.add).then_inc(a_sp, 1)
                ve.wait_ge(a_sp, n + 1)
                if n >= 2:
                    ve.wait_ge(a_w, n - 1)
                ve.tensor_tensor_scan(r[:, ::-1], consts[:, K_SEG:K_SEG + 3 * P][:, ::-1], e[:, ::-1], 0.0,
                                      ALU.mult, ALU.add).then_inc(a_scan, 1)

            def read_output(i):
                d, c, at = width(i), head_col(i), place(i)
                ve.wait_ge(a_pv, i + 1)
                if kind(i) != SB:
                    ve.reciprocal(rinv[:, at, :], row[:, at, :]).then_inc(a_ri, 1)
                    ve.wait_ge(a_ri, softmaxes(i) + 1)
                for q in range(2):
                    o, src = o_tok[q][:, c:c + d], ps[1][:, i % 2, q * d:(q + 1) * d]
                    if kind(i) != SB:
                        ins = ve.tensor_scalar(o, src, rinv[:, at, q:q + 1], None, ALU.mult)
                    else:
                        ins = ve.tensor_copy(o, src)
                ins.then_inc(a_o, 1)

            def sum_squares(i):
                d = width(i)
                ve.wait_ge(a_sq, i + 1)
                ve.tensor_reduce(hss[:, place(i), :], osq[i % 2][:, 0:2 * d].rearrange("p (q d) -> p q d", q=2),
                                 AX.X, ALU.add).then_inc(a_ss, 1)

            for t in range(STEPS + 1):
                if 0 <= t - MASK < HEADS:
                    masked_scores(t - MASK)
                if 0 <= t - STICK < HEADS and kind(t - STICK) == SB:
                    stick_sums(t - STICK)
                if 0 <= t - READ < HEADS:
                    read_output(t - READ)
                if 0 <= t - SUM < HEADS:
                    sum_squares(t - SUM)
                for j in range(min(CPS, CPS * t // (STEPS - 4)), min(CPS, CPS * (t + 1) // (STEPS - 4))):
                    add_chunk(A_SHM, 0, Z_SHM, 0, 0, j)
            ve.wait_ge(a_ss, HEADS)
            narrow = hss[:, 0:2 * H, :]
            ve.tensor_scalar(narrow, narrow, 1.0 / DH, EPS, ALU.mult, ALU.add)
            ve.tensor_scalar(hss[:, 2 * H:HEADS, :], hss[:, 2 * H:HEADS, :], 1.0 / VD, EPS, ALU.mult,
                             ALU.add).then_inc(ms_s, 1)
            ve.wait_ge(rt_s, 3)
            ve.reciprocal(hss[:, :, :], hss[:, :, :]).then_inc(a_ri, 1)
            ve.wait_ge(a_ri, 2 * H + 1)
            for first, n, d, c, tiles in ((2 * H, H, VD, 0, (0, 1)), (0, 2 * H, DH, H * VD, (0,))):
                for q in tiles:
                    o = o_tok[q][:, c:c + n * d].rearrange("p (h d) -> p h d", d=d)
                    ve.tensor_tensor(o, o, hss[:, first:first + n, q].unsqueeze(2).to_broadcast([P, n, d]),
                                     ALU.mult).then_inc(a_n, 1)
            for j in range(8):
                use = USE_OT + j // 4
                ve.wait_ge(op_hi, R_O + j + 1)
                for k in range(2):
                    c = C_OUT + 2 * j + k
                    ins = ve.scalar_tensor_tensor(
                        out=hT[:, 2 * j + k, 1, :], in0=ps[use % 2][:, j % 4, k * S:(k + 1) * S],
                        scalar=cols[:, c:c + 1], in1=hT[:, 2 * j + k, 0, :].bitcast(F32),
                        op0=ALU.mult, op1=ALU.subtract)
                ins.then_inc(op_lo, 1)
                if j % 4 == 3:
                    ve.wait_ge(op_lo, R_O + j + 1)
                    ve.sem_inc(psum_free, 1)

            ve.wait_ge(psum_ready, READY[USE_SHM])
            read_mod(USE_SHM, 0, SH_M).then_inc(mod_s, 1)
            ve.wait_ge(mod_s, 10)
            ve.sem_inc(psum_free, 1)
            clear_acc((0, 2), A_SCM, Z_SCM)
            for b in range(4):
                for j in range(8 * b, 8 * b + 8):
                    lo(B_OUT + LAG, 0, 0, j)
                    add_chunk(A_SCM, 0, Z_SCM, 0, 0, j)
                gate_block(USE_OUT + b, B_OUT + 8 * b + 8, 0, b, 4 * b, G_A, 0)
            ve.wait_ge(psum_ready, READY[USE_FFN])
            read_mod(USE_FFN, 0, SC_M).then_inc(mod_s, 1)
            ve.wait_ge(mod_s, 11)
            make_gain(SC_M, C_FFN)
            ve.wait_ge(gain_s, 5)
            ve.wait_ge(psum_ready, READY["ffn norm"])
            mean(USE_FFN, 1, 0, D).then_inc(ms_s, 1)
            ve.wait_ge(ms_s, 4)
            ve.sem_inc(psum_free, 1)
            invert(4, 3)
            modulated_norm(R_FFN, SH_M, 0, 8)
            clear_acc((0, 2), A_GM, Z_GM)

            for half in range(2):
                base = B_FF + half * (U_FF1 + U_FF2)
                use1, e1 = ((USE_FF1A, E_FF1A), (USE_FF1B, E_FF1B))[half]
                with ve.Fori(0, 4) as it:
                    for b in range(2):
                        for j in range(8 * b, 8 * b + 8):
                            lo(base + LAG, 16, it, j)
                            if half == 0 and j % 2 == 1:
                                add_chunk(A_GM, 0, Z_GM, 8, it, 4 * b + j % 8 // 2)
                        sum_halves(tmp2[:, :, :], use1 + b, 2, e1 + b, 2, it, psum_free)
                        ve.wait_ge(psum_free, use1 + b + 2 + 2 * it)
                        ve.scalar_tensor_tensor(out=tmp2[:, :, :], in0=tmp2[:, :, :], scalar=0.0,
                                                in1=tmp2[:, :, :], op0=ALU.max, op1=ALU.mult).then_inc(relu2, 1)
                        blk = bass.ds(4 * b + 8 * it, 4)
                        ve.wait_ge(act_hi, 8 * half + b + 1 + 2 * it)
                        ve.tensor_tensor(act[:, blk, 1, :], tmp2[:, :, :], act[:, blk, 0, :].bitcast(F32),
                                         ALU.subtract).then_inc(act_lo, 1)
                use2 = (USE_FF2A, USE_FF2B)[half]
                if half == 0:
                    ve.wait_ge(psum_ready, READY[USE_GM])
                    read_mod(USE_GM, 0, G_M).then_inc(mod_s, 1)
                    ve.wait_ge(mod_s, 12)
                    ve.sem_inc(psum_free, 1)

                def down(it, last=False):
                    for b in range(2):
                        for j in range(16):
                            if not (last and b == 1 and j >= 16 - LAG):
                                lo(base + U_FF1 + LAG, 32, it, 16 * b + j)
                        gate_block(use2 + b, base + U_FF1 + 16 * b + 16, 32, 4 + 4 * half + b,
                                   4 * b + 8 * it, G_M, it)

                if half == 0:
                    with ve.Fori(0, 2) as it:
                        down(it)
                else:
                    down(0)
                    down(1, last=True)
            ve.wait_ge(psum_ready, READY[USE_END])
            mean(USE_END, 0, 0, D).then_inc(ms_s, 1)
            invert(5, 4)
            for k in range(KT):
                dst = (tmp, tmp2, sq, ssq)[k // 4]
                ve.scalar_tensor_tensor(out=dst[:, k % 4, :], in0=xT[:, k, :], scalar=cols[:, C_FIN + k:C_FIN + k + 1],
                                        in1=rstd[:, 0, :], op0=ALU.mult, op1=ALU.mult).then_inc(fin_s, 1)

        @block.tensor
        def _(pe):
            def take(use, n_use=0, it=0):
                if use >= 1:
                    pe.wait_ge(psum_free, use + n_use * it)

            def unit(u0, step, it, j, out_set, rhs, kt0, ready, first, last):
                slot = (u0 + j) % RING
                pe.wait_ge(*ready)
                pe.wait_ge(hi_done, u0 + j + 1 + step * it)
                for k in range(UK):
                    for n in range(4):
                        pe.matmul(out_set[:, n, :], w_hi[:, slot, k, n * P:(n + 1) * P], rhs[:, kt0 + k, :, :],
                                  start=first and k == 0, stop=False)
                pe.wait_ge(lo_sem(u0 + j), lo_count(u0, step, it, j))
                for k in range(UK):
                    for n in range(4):
                        ins = pe.matmul(out_set[:, n, 0:S], w_lo[:, slot, k, n * P:(n + 1) * P],
                                        rhs[:, kt0 + k, 0, :], start=False, stop=last and k == UK - 1)
                ins.then_inc(unit_used, 1)

            def product(u0, step, it, j0, units, use, n_use, rhs, kt0, ready):
                take(use, n_use, it)
                for j in range(units):
                    unit(u0, step, it, j0 + j, ps[use % 2], rhs, kt0 + UK * j, ready(j), j == 0, j == units - 1)

            def column_sums(use, k0=0, n=KT):
                for k in range(n):
                    ins = pe.matmul(ps[use % 2][:, 0, k:k + 1], accA[:, (k0 + k) * P:(k0 + k + 1) * P],
                                    ones[:, 0:1], start=True, stop=True)
                ins.then_inc(psum_ready, 1)

            def token_sums(use, bank, src, n):
                for k in range(n):
                    ins = pe.matmul(ps[use % 2][:, bank, 0:S], ones, src[:, k, :], start=(k == 0), stop=(k == n - 1))
                return ins

            def residual_sums(use, bank, added, squares):
                s = ps[use % 2][:, bank, 0:S]
                pe.wait_ge(ssq_done, added)
                for k in range(4):
                    pe.matmul(s, ones, ssq[:, k, :], start=(k == 0), stop=False)
                for k in range(4):
                    pe.wait_ge(sq_done, squares + k + 1)
                    ins = pe.matmul(s, ones, sq[:, k, :], start=False, stop=(k == 3))
                ins.then_inc(psum_ready, 1)

            pe.wait_ge(ld_cols, 16)
            pe.wait_ge(ssq_done, 4)
            token_sums(0, 1, ssq, 4)
            for q in range(4):
                take(9 * q)
                pe.wait_ge(acc_done, QC * (q + 1) + Z_Q(q))
                column_sums(9 * q, q % 2 * 8, 8)
                with pe.Fori(0, 4) as it:
                    for b in range(2):
                        product(QC * q, 4, it, 2 * b, 2, use_in(q, b), 2, hT, QT * q,
                                lambda j: (op_lo, R_MIX + 2 * q + j + 1))
            take(USE_LSTAT)
            pe.wait_ge(sq_done, 5)
            token_sums(USE_LSTAT, 0, tmp2, 4).then_inc(lsq, 1)
            pe.wait_ge(sq_done, 6)
            token_sums(USE_LSTAT, 1, tmp2, 2).then_inc(psum_ready, 1)
            for n in range(3):
                product(B_LAT, 0, 0, 2 * n, 2, USE_LAT + n, 0, lat, 0, lambda j: (op_lo, R_CQ + j + 1))
            for n in range(4):
                product(B_LAT, 0, 0, U_UQ + n, 1, USE_LAT + 3 + n, 0, lat, 4, lambda j: (op_lo, R_CKV + 1))
            pe.wait_ge(ld_const, 16)
            take(USE_ROT)
            rotate = consts[:, K_ROT:K_ROT + P]
            for b in range(2):
                pe.matmul(ps[USE_ROT % 2][:, b, :], rotate, rope_raw[:, 2 * b:2 * b + 2, :], start=True, stop=True)
            pe.matmul(ps[USE_ROT % 2][:, 2, 0:S], rotate, pT[:, T_KR, :], start=True, stop=True)\
                .then_inc(psum_ready, 1)
            pe.wait_ge(psum_free, USE_LAT + 8)
            for t in range(2):
                for k in range(H):
                    ins = pe.transpose(ps[USE_VM % 2][:, 2 * t + k // 4, (k % 4) * P:(k % 4 + 1) * P],
                                       vT[:, k, t * P:(t + 1) * P], ident)
            ins.then_inc(psum_ready, 1)
            take(USE_VS)
            for g, t0 in ((0, T_SB + 8), (1, T_FX + 8)):
                for t in range(2):
                    for k in range(4):
                        ins = pe.transpose(ps[USE_VS % 2][:, 2 * g + t, k * P:(k + 1) * P],
                                           pT[:, t0 + k, t * P:(t + 1) * P], ident)
            ins.then_inc(psum_ready, 1)

            take(USE_GA)
            pe.wait_ge(acc_done, A_SHM + Z_GA)
            column_sums(USE_GA)

            def scores(i):
                s = ps[0][:, i % 2, :]
                n, tile, r = i // 3, i // 3 // 2, DH * (i // 3 % 2)
                if kind(i) != ML:
                    t0 = (T_SB if kind(i) == SB else T_FX) + tile
                    terms = [(pT[r:r + DH, t0, :], pT[r:r + DH, t0 + 4, :])]
                    if kind(i) == FX:
                        terms.append((foxA[:, :], foxB[:, n % 2, :]))
                else:
                    terms = [(q_nope[:, n, :], k_nope[:, n, :]),
                             (q_rope[r:r + DH, tile, :], pT[r:r + DH, T_KR, :])]
                if i >= 2:
                    pe.wait_ge(a_zm, i - 1)
                if kind(i) == FX:
                    pe.wait_ge(fb_s, n + 1)
                for q in range(2):
                    for m, (lhs, rhs) in enumerate(terms):
                        ins = pe.matmul(s[:, q * P:(2 * q + 1) * P],
                                        lhs[:, q * P:(q + 1) * P], rhs[:, 0:(q + 1) * P],
                                        start=(m == 0), stop=(m == len(terms) - 1))
                ins.then_inc(a_sc, 1)

            def transpose_p(i):
                pe.wait_ge(a_p, i + 1)
                if i >= 2:
                    pe.wait_ge(a_pt, i - 1)
                for b in range(3):
                    ins = pe.transpose(ps[0][:, 2 + i % 2, b * P:(b + 1) * P], probs[i % 2][:, b * P:(b + 1) * P],
                                       ident)
                ins.then_inc(a_tr, 1)

            def weigh_v(i):
                d, n = width(i), i // 3
                v = (v_sb, v_mla, v_fx)[kind(i)][:, :, n * d:(n + 1) * d]
                pe.wait_ge(a_pt, i + 1)
                if i >= 2:
                    pe.wait_ge(a_o, i - 1)
                o, pt = ps[1][:, i % 2, :], probsT[i % 2]
                pe.matmul(o[:, 0:d], pt[:, 0:P], v[:, 0, :], start=True, stop=True)
                pe.matmul(o[:, d:2 * d], pt[:, P:2 * P], v[:, 0, :], start=True, stop=False)
                pe.matmul(o[:, d:2 * d], pt[:, 2 * P:3 * P], v[:, 1, :], start=False, stop=True).then_inc(a_pv, 1)

            pe.wait_ge(psum_free, USE_GA + 2)
            pe.wait_ge(q_sc, 2)
            pe.wait_ge(rope_c, 2)
            pe.wait_ge(fg_s, 1)
            pe.wait_ge(fm_s, 4)
            for t in range(STEPS):
                if t < HEADS:
                    scores(t)
                if 0 <= t - TURN < HEADS:
                    transpose_p(t - TURN)
                if 0 <= t - MIX < HEADS:
                    weigh_v(t - MIX)
            for k in range(KT):
                use = USE_OT + k // 8
                pe.wait_ge(a_n, 2 + k // 8)
                if k >= 8:
                    pe.wait_ge(a_np, 1)
                for q in range(2):
                    c = (k % 2) * S + q * P
                    ins = pe.transpose(ps[use % 2][:, k % 8 // 2, c:c + P], o_tok[q][:, k * P:(k + 1) * P], ident)
                if k % 8 == 7:
                    ins.then_inc(psum_ready, 1)
            take(USE_SHM)
            pe.wait_ge(acc_done, A_SCM + Z_SHM)
            column_sums(USE_SHM)
            for b in range(4):
                product(B_OUT, 0, 0, 8 * b, 8, USE_OUT + b, 0, hT, 0, lambda j: (op_lo, R_O + j + 1))
            take(USE_FFN)
            pe.wait_ge(acc_done, A_GM + Z_SCM)
            column_sums(USE_FFN)
            residual_sums(USE_FFN, 1, 7, 9)
            for half in range(2):
                base = B_FF + half * (U_FF1 + U_FF2)
                use1, use2 = ((USE_FF1A, USE_FF2A), (USE_FF1B, USE_FF2B))[half]
                with pe.Fori(0, 4) as it:
                    for b in range(2):
                        product(base, 16, it, 8 * b, 8, use1 + b, 2, hT, 0, lambda j: (op_lo, R_FFN + j + 1))
                if half == 0:
                    take(USE_GM)
                    pe.wait_ge(acc_done, A_GM + CPS + Z_GM)
                    column_sums(USE_GM)
                with pe.Fori(0, 2) as it:
                    for b in range(2):
                        product(base + U_FF1, 32, it, 16 * b, 16, use2 + b, 2, act, 0,
                                lambda j: (act_lo, 8 * half + j // 2 + 1))
            take(USE_END)
            residual_sums(USE_END, 0, 10, 16)


def feature_columns(v):
    return np.asarray(v).reshape(-1, P).T


def shape_constants():
    c = np.zeros((P, K_END), np.float32)
    c[:, K_ID:K_ID + P] = np.eye(P, dtype=np.float32)
    m = np.arange(P)
    low = m % ROPE < ROPE // 2
    c[m[low] + ROPE // 2, K_ROT + m[low]] = -1.0
    c[m[~low] - ROPE // 2, K_ROT + m[~low]] = 1.0
    inv = np.float32(ROPE_BASE) ** (-np.arange(0, ROPE, 2, dtype=np.float32) / np.float32(ROPE))
    ang = np.arange(S, dtype=np.float32)[None, :] * inv[m % (ROPE // 2)][:, None]
    c[:, K_COS:K_COS + S] = np.cos(ang)
    c[:, K_SIN:K_SIN + S] = np.sin(ang)
    q, k = m[:, None], m[None, :]
    for at, allowed in ((K_FOX, k <= q), (K_SB, k < q), (K_MLA, k < (q // CHUNK + 1) * CHUNK)):
        diagonal = np.where(allowed, 0.0, MASKED)
        c[:, at:at + P] = diagonal
        c[:, at + 2 * P:at + 3 * P] = diagonal
    c[:, K_SEG:K_SEG + 3 * P] = 1.0
    c[:, [K_SEG + P - 1, K_SEG + 3 * P - 1]] = 0.0
    for n in range(H):
        c[[n, 32 + n], K_SEL + n] = 1.0
    return c


def units_of(w):
    k, n = w.shape
    return w.reshape(k // (UK * P), UK, P, n // BW, BW).transpose(3, 0, 2, 1, 4).reshape(-1, P, UC)


def kernel(x, c, w_ada, b_ada, norm_mix, w_in, q_norm, w_uq, kv_norm, w_ukv, b_forget,
           out_norm, w_out, norm_ffn, w_ff1, w_ff2, final_norm):
    import concourse.bacc as bacc
    from concourse.bass_utils import run_bass_kernel_spmd

    f32 = np.float32
    a = lambda v: np.asarray(v)
    w_in, w_uq, w_ukv, w_ff1, w_ff2 = (a(w)[0] for w in (w_in, w_uq, w_ukv, w_ff1, w_ff2))
    lat = QL + KVL
    rope, gates = w_in[:, lat:lat + ROPE], w_in[:, -H:]
    pad = np.zeros((D, P - H), f32)
    w_in = np.concatenate([w_in[:, :lat], rope, rope, gates, pad, w_in[:, lat + ROPE:-H]], axis=1)
    uq = w_uq.reshape(QL, H, NOPE + ROPE)
    ukv = w_ukv.reshape(KVL, H, NOPE + VD)
    parts = [w_in[q * QT * P:(q + 1) * QT * P] for q in range(4)]
    parts += [
             uq[:, :, :NOPE].reshape(QL, -1), uq[:, :, NOPE:].reshape(QL, -1),
             ukv[:, :, :NOPE].reshape(KVL, -1), ukv[:, :, NOPE:].reshape(KVL, -1), a(w_out)[0]]
    for h in range(2):
        parts += [w_ff1[:, h * FF // 2:(h + 1) * FF // 2], w_ff2[h * FF // 2:(h + 1) * FF // 2]]
    weights = np.concatenate([units_of(w) for w in parts])
    ada = a(w_ada)[0].reshape(KT, P, 6, D)
    first = [np.concatenate([ada[:, :, g, q * QT * P:(q + 1) * QT * P] for g in (SC_A, SH_A)], axis=-1)
             for q in range(4)]
    later = [ada[:, :, g].reshape(KT, P, D // AC, AC).transpose(0, 2, 1, 3).reshape(-1, P, AC)
             for g in (G_A, SH_M, SC_M, G_M)]
    ada = np.concatenate(first + later)
    cols = np.zeros((P, C_END), f32)
    for at, v in ((C_C, c), (C_B, a(b_ada)[0]), (C_MIX, a(norm_mix)[0]), (C_FFN, a(norm_ffn)[0]),
                  (C_OUT, a(out_norm)[0]), (C_FIN, final_norm), (C_QN, a(q_norm)[0]), (C_KVN, a(kv_norm)[0])):
        v = feature_columns(v)
        cols[:, at:at + v.shape[1]] = v
    cols[:H, C_BF] = a(b_forget)[0]
    cols[:, C_ONE:] = 1.0
    xt = a(x)[0].reshape(S, KT, P).transpose(2, 1, 0).reshape(P, -1)
    arrays = {"xt": xt, "cols": cols, "consts": shape_constants(), "ada": ada, "weights": weights}
    arrays = {n: np.ascontiguousarray(v) for n, v in arrays.items()}

    nc = bacc.Bacc("TRN2", target_bir_lowering=False, num_devices=1)
    aps = [nc.dram_tensor(f"in_{n}", v.shape, F32, kind="ExternalInput").ap() for n, v in arrays.items()]
    y = nc.dram_tensor("y", (P, KT * S), F32, kind="ExternalOutput").ap()
    hybrid_block(nc, *aps, y)
    r = run_bass_kernel_spmd(nc, [{f"in_{n}": v for n, v in arrays.items()}], core_ids=[0])
    got = r.results[0]["y"]
    return np.ascontiguousarray(got.reshape(P, KT, S).transpose(2, 1, 0).reshape(1, S, D))
```

```python
from contextlib import ExitStack

import numpy as np
import concourse.bass as bass
from concourse import mybir

P = 128
D, S, FF = 2048, 256, 8192
EPS = 1e-6
KT = D // P
H, QL, KVL, NOPE, ROPE, VD = 8, 512, 256, 128, 64, 128
DH = 64
CHUNK, ROPE_BASE = 64, 10000.0
MASKED = -1e30
BW = 512
UK = 2
UC = UK * BW
RING = 4
LAG = RING
AHEAD = LAG + RING

U_IN = 8 * (KT // UK)
U_UQ, U_UKV = 3 * (QL // P // UK), 4 * (KVL // P // UK)
U_LAT = U_UQ + U_UKV
LAT_ENDS = [1, 3, 5, 6, 7, 8, 9]
U_OUT = (D // BW) * (KT // UK)
HALF = FF // 2 // P
U_FF1 = (FF // 2 // BW) * (KT // UK)
U_FF2 = (D // BW) * (HALF // UK)
B_LAT = U_IN
B_OUT = B_LAT + U_LAT
B_FF = B_OUT + U_OUT
UNITS = B_FF + 2 * (U_FF1 + U_FF2)

AC = 1024
CPS = KT * (D // AC)
ADA = 4
SH_A, SC_A, G_A, SH_M, SC_M, G_M = range(6)
QT = KT // 4
QC = KT
A_GA, A_SHM, A_SCM, A_GM = (4 * QC + n * CPS for n in range(4))
Z_Q, Z_GA, Z_SHM, Z_SCM, Z_GM = (lambda q: q + 1), 5, 6, 7, 8

def use_in(q, blk):
    return 9 * q + 1 + blk


USE_LSTAT = 36
USE_LAT = 37
USE_ROT, USE_VM, USE_VS, USE_GA = 44, 45, 46, 47
USE_OT = 48
USE_SHM = 50
USE_OUT = 51
USE_FFN = 55
USE_FF1A, USE_GM, USE_FF2A = 56, 64, 65
USE_FF1B, USE_FF2B, USE_END = 69, 77, 81
READY = {use: n + 1 for n, use in enumerate((
    0, 9, 18, 27, USE_LSTAT, USE_ROT, USE_VM, USE_VS, USE_GA, USE_OT, USE_OT + 1, USE_SHM,
    USE_FFN, "ffn norm", USE_GM, USE_END))}
E_LAT, E_FF1A, E_FF1B = 32, 39, 47

R_MIX, R_CQ, R_CKV, R_O, R_FFN = 0, 8, 10, 11, 19

C_C, C_B, C_MIX, C_FFN, C_OUT, C_FIN, C_QN, C_KVN, C_BF, C_ONE = np.cumsum(
    [0, KT, 6 * KT, KT, KT, KT, KT, QL // P, KVL // P, 1]).tolist()
C_END = C_ONE + P
K_ID, K_ROT, K_COS, K_SIN, K_FOX, K_SB, K_MLA, K_SEG, K_SEL = np.cumsum(
    [0, P, P, S, S, 3 * P, 3 * P, 3 * P, 3 * P]).tolist()
K_END = K_SEL + H

F32, F32R = mybir.dt.float32, mybir.dt.float32r
ALU, ACT, AX = mybir.AluOpType, mybir.ActivationFunctionType, mybir.AxisListType

SB, ML, FX, HEADS = 0, 1, 2, 3 * H


def kind(i):
    return i % 3


def place(i):
    return (0, 2, 1)[kind(i)] * H + i // 3


def width(i):
    return VD if kind(i) == ML else DH


def softmaxes(i):
    return i - (i + 2) // 3


SCORE, MASK, SOFT, STICK, WEIGH, TURN, COPY, MIX, READ, SUM = range(10)
STEPS = HEADS + SUM
ZM = WEIGH - MASK + 1

T_CQ, T_CKV, T_KR, T_F, T_SB, T_FX = 0, 4, 6, 7, 8, 20


def hybrid_block(nc, xt_in, cols_in, consts_in, w_ada, weights, out):
    ctx = ExitStack()
    with ctx:
        def sb(name, shape, dt=F32, at=ctx):
            return at.enter_context(nc.sbuf_tensor(name, shape, dt))

        def sem(name):
            return ctx.enter_context(nc.semaphore(name))

        raw = sb("raw", [P, RING, UK, BW])
        w_hi = sb("w_hi", [P, RING, UK, BW], F32R)
        w_lo = sb("w_lo", [P, RING, UK, BW], F32R)
        xT = sb("xT", [P, KT, S])
        ada = sb("ada", [P, ADA, AC])
        accA = sb("accA", [P, D])
        tmp = sb("tmp", [P, 4, S])
        tmp2 = sb("tmp2", [P, 4, S])
        cols = sb("cols", [P, C_END])
        mod = sb("mod", [P, 6, KT])
        c_act = sb("c_act", [P, KT])
        gain = sb("gain", [P, KT])
        rstd = sb("rstd", [P, 2, S])
        small = sb("small", [P, 4 * KT])
        row = sb("row", [P, HEADS, 2])
        rinv = sb("rinv", [P, HEADS, 2])
        hss = sb("hss", [P, HEADS, 2])
        mx = sb("mx", [P, HEADS, 2])
        with ExitStack() as r:
            q_nope = sb("q_nope", [P, H, S], F32, r)
            k_nope = sb("k_nope", [P, H, S], F32, r)
            q_rope = sb("q_rope", [P, H // 2, S], F32, r)
            rope_raw = sb("rope_raw", [P, H // 2, S], F32, r)
            with ExitStack() as v:
                vT = sb("vT", [P, H, S], F32, v)
            o_tok0 = sb("o_tok0", [P, D], F32, r)
        hT = sb("hT", [P, KT, 2, S], F32R)
        with ExitStack() as r:
            foxA = sb("foxA", [P, S], F32, r)
            foxG = sb("foxG", [P, S], F32, r)
            foxB = sb("foxB", [P, 2, S], F32, r)
            pT = sb("pT", [P, 32, S], F32, r)
            consts = sb("consts", [P, K_END], F32, r)
            v_mla = sb("v_mla", [P, 2, H * VD], F32, r)
            o_tok1 = sb("o_tok1", [P, D], F32, r)
            with ExitStack() as v:
                lat = sb("lat", [P, 6, 2, S], F32R, v)
            zm = sb("zm", [P, ZM, 3 * P], F32, r)
            el = sb("el", [P, 2, 3 * P], F32, r)
            stick = sb("stick", [P, 2, 3 * P], F32, r)
        act = sb("act", [P, HALF, 2, S], F32R)
        ssq = sb("ssq", [P, 4, S])
        sq = sb("sq", [P, 4, S])
        v_sb = pT[:, T_CQ:T_CQ + 4, :].rearrange("p a b -> p (a b)").rearrange("p (t n) -> p t n", t=2)
        v_fx = pT[:, T_SB + 8:T_SB + 12, :].rearrange("p a b -> p (a b)").rearrange("p (t n) -> p t n", t=2)
        o_tok = [o_tok0, o_tok1]
        ones = cols[:, C_ONE:C_ONE + P]
        ident = consts[:, K_ID:K_ID + P]

        def scratch(t):
            return t[:, :, :].rearrange("p a b -> p (a b)")

        probs = [scratch(tmp)[:, i * 384:i * 384 + 384] for i in range(2)]
        probsT = [scratch(tmp2)[:, i * 384:i * 384 + 384] for i in range(2)]
        osq = [scratch(t)[:, 768:1024] for t in (tmp, tmp2)]

        ps = [ctx.enter_context(nc.psum_tensor(f"ps{i}", [P, 4, 512], F32)) for i in range(2)]

        ld_cols, ld_x, ld_const, ld_out = sem("ld_cols"), sem("ld_x"), sem("ld_const"), sem("ld_out")
        raw_full = [sem(f"raw_full{i}") for i in range(RING)]
        ada_full = [sem(f"ada_full{i}") for i in range(ADA)]
        hi_done = sem("hi_done")
        lo_vec, lo_pool = sem("lo_vec"), sem("lo_pool")
        unit_used = sem("unit_used")
        psum_ready = sem("psum_ready")
        psum_free = sem("psum_free")
        tmp_ready = sem("tmp_ready")
        acc_done = sem("acc_done")
        silu_step = sem("silu_step")
        mod_ready = sem("mod_ready")
        gain_ready = sem("gain_ready")
        x_half = sem("x_half")
        zeroed = sem("zeroed")
        part_added = sem("part_added")
        x_new = sem("x_new")
        sq_done = sem("sq_done")
        ssq_done = sem("ssq_done")
        mean_done, root_done, rstd_ready = sem("mean_done"), sem("root_done"), sem("rstd_ready")
        t_ready = sem("t_ready")
        op_hi, op_lo = sem("op_hi"), sem("op_lo")
        relu2 = sem("relu2")
        act_hi, act_lo = sem("act_hi"), sem("act_lo")
        cq_summed = sem("cq_summed")
        rope_term, rope_done = sem("rope_term"), sem("rope_done")
        v_copied = sem("v_copied")
        forget_step = sem("forget_step")
        neg_f_ready = sem("neg_f_ready")
        fox_filled = sem("fox_filled")
        fox_b_ready = sem("fox_b_ready")
        q_scaled = sem("q_scaled")
        scores_done = sem("scores_done")
        masked = sem("masked")
        max_done = sem("max_done")
        abs_done, exp_done, ln_done = sem("abs_done"), sem("exp_done"), sem("ln_done")
        softplus_done, stick_done, log_p_done = sem("softplus_done"), sem("stick_done"), sem("log_p_done")
        probs_ready, probs_turned, probs_copied = sem("probs_ready"), sem("probs_turned"), sem("probs_copied")
        out_ready = sem("out_ready")
        inverse_done = sem("inverse_done")
        out_read, out_squared, out_summed = sem("out_read"), sem("out_squared"), sem("out_summed")
        normed_vec, normed_pool = sem("normed_vec"), sem("normed_pool")
        result_ready = sem("result_ready")

        block = ctx.enter_context(nc.Block())

        def lo_count(u0, step, it, j):
            return (u0 + j) // 2 + 1 + (step // 2) * it

        def lo_sem(u):
            return lo_vec if u % 2 == 0 else lo_pool

        def scaled(n):
            return n - 8 if n >= R_FFN else n

        def head_col(i):
            return VD * (i // 3) if kind(i) == ML else H * VD + DH * place(i)

        @block.sync
        def _(sp):
            def load_unit(u0, step, it, j, fresh=False):
                if not fresh:
                    sp.wait_ge(lo_sem(u0 + j), lo_count(u0 - RING, step, it, j))
                slot = (u0 + j) % RING
                sp.dma_start(raw[:, slot, :, :].rearrange("p k n -> p (k n)"),
                             weights[u0 + j + step * it, :, :]).then_inc(raw_full[slot], 16)

            def load_ada(a0, zeros, step, it, j, fresh=False):
                if not fresh:
                    sp.wait_ge(acc_done, a0 + j - ADA + 1 + zeros + step * it)
                slot = (a0 + j) % ADA
                sp.dma_start(ada[:, slot, :], w_ada[a0 + j + step * it, :, :]).then_inc(ada_full[slot], 16)

            sp.dma_start(cols[:, :], cols_in).then_inc(ld_cols, 16)
            for j in range(ADA):
                load_ada(0, 0, 0, 0, j, fresh=True)
            sp.dma_start(xT[:, :, :].rearrange("p k t -> p (k t)"), xt_in).then_inc(ld_x, 16)
            for j in range(8):
                load_ada(ADA, Z_Q(0), 0, 0, j)
            for j in range(RING):
                load_unit(0, 0, 0, j, fresh=True)
            for j in range(4):
                load_ada(12, Z_Q(0), 0, 0, j)
            for j in range(4):
                load_ada(QC, Z_Q(0), 0, 0, j)
            for j in range(RING):
                load_unit(RING, 0, 0, j)
            for q in range(4):
                if q == 3:
                    sp.dma_start(consts[:, :], consts_in).then_inc(ld_const, 16)
                with sp.Fori(0, QC // 4) as it:
                    for j in range(RING):
                        load_unit(QC * q + AHEAD, RING, it, j)
                        load_ada(QC * (q + 1) + ADA, Z_Q(q + 1), ADA, it, j)
            loaded = AHEAD
            for n in range(8):
                if n < 7:
                    for u in range(loaded, LAT_ENDS[n] + 1 + AHEAD):
                        load_unit(B_LAT, 0, 0, u)
                    loaded = LAT_ENDS[n] + 1 + AHEAD
                for j in range(2):
                    load_ada(A_GA + QC + ADA + 2 * n, Z_GA, 0, 0, j)
            with sp.Fori(0, CPS // ADA) as it:
                for j in range(ADA):
                    load_ada(A_SHM + ADA, Z_SHM, ADA, it, j)
            for j in range(ADA):
                load_ada(A_SCM + ADA, Z_SCM, 0, 0, j)
            with sp.Fori(0, U_OUT // RING - 1) as it:
                for j in range(RING):
                    load_unit(B_OUT + AHEAD, RING, it, j)
                    load_ada(A_SCM + 2 * ADA, Z_SCM, RING, it, j)
            for j in range(RING):
                load_unit(B_OUT + AHEAD + U_OUT - RING, 0, 0, j)
            with sp.Fori(0, CPS // 4 - 1) as it:
                for j in range(8):
                    load_unit(B_FF + AHEAD, 8, it, j)
                    if j % 2 == 1:
                        load_ada(A_GM + ADA, Z_GM, ADA, it, j // 2)
            rest = B_FF + AHEAD + 2 * (CPS - ADA)
            with sp.Fori(0, (UNITS - rest) // RING) as it:
                for j in range(RING):
                    load_unit(rest, RING, it, j)
            for j in range(4):
                sp.wait_ge(result_ready, 4 * j + 4)
                src = (tmp, tmp2, sq, ssq)[j]
                sp.dma_start(out[:, 4 * j * S:(4 * j + 4) * S], scratch(src)).then_inc(ld_out, 16)
            sp.wait_ge(ld_out, 64)

        @block.scalar
        def _(sc):
            def hi(u0, step, it, j):
                slot = (u0 + j) % RING
                sc.wait_ge(raw_full[slot], 16 * ((u0 + j) // RING + 1) + (16 * step // RING) * it)
                if u0 + j >= RING:
                    sc.wait_ge(unit_used, u0 + j - RING + 1 + step * it)
                sc.activation(w_hi[:, slot, :, :], raw[:, slot, :, :], ACT.Copy).then_inc(hi_done, 1)

            def copy_low(use, used, step, it):
                sc.wait_ge(unit_used, used + step * it)
                sc.wait_ge(psum_free, use + 1 + 2 * it)
                sc.activation(tmp[:, :, :], ps[use % 2][:, :, S:2 * S], ACT.Copy).then_inc(tmp_ready, 1)

            def square(blocks, it, blk, added):
                sc.wait_ge(x_new, 4 * blocks + 8 * it)
                sc.wait_ge(ssq_done, added)
                sc.activation(sq[:, :, :], xT[:, bass.ds(blk, 4), :], ACT.Square).then_inc(sq_done, 1)

            def square_tiles(blocks, added):
                sc.wait_ge(ssq_done, added)
                for n in range(4):
                    sc.wait_ge(x_new, 4 * blocks - 3 + n)
                    sc.activation(sq[:, n, :], xT[:, KT - 4 + n, :], ACT.Square).then_inc(sq_done, 1)

            def root(n, halves=1):
                sc.wait_ge(mean_done, n)
                sc.activation(rstd[:, 0:halves, :], rstd[:, 0:halves, :], ACT.Sqrt).then_inc(root_done, 1)

            def operand_hi(n, dst, bias):
                sc.wait_ge(t_ready, scaled(n) + 1)
                t = tmp[:, 2 * (n % 2):2 * (n % 2) + 2, :]
                if bias is None:
                    sc.activation(dst[:, :, 0, :], t, ACT.Copy).then_inc(op_hi, 1)
                else:
                    sc.activation(dst[:, 0, 0, :], t[:, 0, :], ACT.Identity, bias=bias[:, 0:1])
                    sc.activation(dst[:, 1, 0, :], t[:, 1, :], ACT.Identity, bias=bias[:, 1:2]).then_inc(op_hi, 1)

            sc.wait_ge(ld_cols, 16)
            sc.activation(c_act[:, :], cols[:, C_C:C_C + KT], ACT.Exp, scale=-1.0).then_inc(silu_step, 1)
            sc.wait_ge(ld_x, 16)
            for b in range(4):
                if b:
                    sc.wait_ge(ssq_done, b)
                sc.activation(sq[:, :, :], xT[:, 4 * b:4 * b + 4, :], ACT.Square).then_inc(sq_done, 1)
            for j in range(RING):
                hi(0, 0, 0, j)
            root(1)
            for q in range(4):
                sc.wait_ge(mod_ready, 2 * q + 2)
                for j in range(2 * q, 2 * q + 2):
                    operand_hi(R_MIX + j, hT[:, 2 * j:2 * j + 2, :, :], mod[:, SH_A, 2 * j:2 * j + 2])
                with sc.Fori(0, 4) as it:
                    for b in range(2):
                        for j in range(2):
                            hi(QC * q + LAG, 4, it, 2 * b + j)
                        copy_low(use_in(q, b), QC * q + 2 * b + 2, 4, it)
            sc.wait_ge(part_added, 33)
            for i, n in ((0, 4), (1, 2)):
                if i:
                    sc.wait_ge(cq_summed, 1)
                sc.activation(tmp2[:, 0:n, :], pT[:, T_CQ + 4 * i:T_CQ + 4 * i + n, :],
                              ACT.Square).then_inc(sq_done, 1)
            root(2, halves=2)
            for n in range(3):
                operand_hi(R_CQ + n, lat[:, 2 * n:2 * n + 2, :, :], None)
            fx = foxB[0:H, 0, :]
            fl = foxB[0:H, 1, :]
            sc.wait_ge(forget_step, 1)
            sc.activation(fl, fx, ACT.Abs).then_inc(forget_step, 1)
            sc.wait_ge(forget_step, 2)
            sc.activation(fl, fl, ACT.Exp, scale=-1.0).then_inc(forget_step, 1)
            sc.wait_ge(forget_step, 3)
            sc.activation(fl, fl, ACT.Ln, bias=cols[0:H, C_ONE:C_ONE + 1]).then_inc(forget_step, 1)
            sc.wait_ge(forget_step, 6)
            sc.activation(foxG[32:32 + H, :], foxA[0:H, :], ACT.Copy, scale=-1.0).then_inc(neg_f_ready, 1)
            for n, e in enumerate(LAT_ENDS):
                for u in range(LAG if n == 0 else LAT_ENDS[n - 1] + 1 + LAG, e + 1 + LAG):
                    hi(B_LAT, 0, 0, u)
                copy_low(USE_LAT + n, B_LAT + e + 1, 0, 0)
            sc.wait_ge(psum_ready, READY[USE_VM])
            sc.activation(v_mla[:, 0, :], ps[USE_VM % 2][:, 0:2, :].rearrange("p a b -> p (a b)"),
                          ACT.Copy).then_inc(v_copied, 1)
            sc.wait_ge(psum_ready, READY[USE_VS])
            sc.activation(v_sb, ps[USE_VS % 2][:, 0:2, :], ACT.Copy).then_inc(v_copied, 1)

            def soft_parts(i):
                n = i // 3
                e = el[:, n % 2, :]
                sc.wait_ge(masked, i + 1)
                if n >= 2:
                    sc.wait_ge(stick_done, n - 1)
                sc.activation(e, zm[:, i % ZM, :], ACT.Abs).then_inc(abs_done, 1)
                sc.wait_ge(abs_done, n + 1)
                sc.activation(e, e, ACT.Exp, scale=-1.0).then_inc(exp_done, 1)
                sc.wait_ge(exp_done, n + 1)
                sc.activation(e, e, ACT.Ln, bias=cols[:, C_ONE:C_ONE + 1]).then_inc(ln_done, 1)

            def weights_of(i):
                p = probs[i % 2]
                if i >= 2:
                    sc.wait_ge(probs_turned, i - 1)
                if kind(i) == SB:
                    sc.wait_ge(log_p_done, i // 3 + 1)
                    sc.activation(p, zm[:, i % ZM, :], ACT.Exp).then_inc(probs_ready, 1)
                else:
                    sc.wait_ge(max_done, 2 * softmaxes(i) + 2)
                    sc.activation(p[:, 0:P], zm[:, i % ZM, 0:P], ACT.Exp, bias=mx[:, place(i), 0:1],
                                  accum_out=row[:, place(i), 0:1])
                    sc.activation(p[:, P:3 * P], zm[:, i % ZM, P:3 * P], ACT.Exp, bias=mx[:, place(i), 1:2],
                                  accum_out=row[:, place(i), 1:2]).then_inc(probs_ready, 1)

            def copy_pt(i):
                sc.wait_ge(probs_turned, i + 1)
                if i >= 2:
                    sc.wait_ge(out_ready, i - 1)
                sc.activation(probsT[i % 2], ps[0][:, 2 + i % 2, 0:3 * P], ACT.Copy).then_inc(probs_copied, 1)

            for t in range(STEPS):
                if 0 <= t - SOFT < HEADS and kind(t - SOFT) == SB:
                    soft_parts(t - SOFT)
                if 0 <= t - WEIGH < HEADS:
                    weights_of(t - WEIGH)
                if 0 <= t - COPY < HEADS:
                    copy_pt(t - COPY)
            sc.wait_ge(mean_done, 3)
            sc.activation(hss[:, :, :], hss[:, :, :], ACT.Sqrt).then_inc(root_done, 1)
            for j in range(8):
                use = USE_OT + j // 4
                if j % 4 == 0:
                    sc.wait_ge(psum_ready, READY[use])
                for k in range(2):
                    c = C_OUT + 2 * j + k
                    ins = sc.activation(hT[:, 2 * j + k, 0, :], ps[use % 2][:, j % 4, k * S:(k + 1) * S],
                                        ACT.Copy, scale=cols[:, c:c + 1])
                ins.then_inc(op_hi, 1)
            for b in range(4):
                for j in range(8):
                    hi(B_OUT + LAG, 0, 0, 8 * b + j)
                if b < 3:
                    square(b + 1, 0, 4 * b, 4 + b)
            square_tiles(4, 7)
            root(4)
            for j in range(8):
                if j == 0:
                    sc.wait_ge(mod_ready, 10)
                operand_hi(R_FFN + j, hT[:, 2 * j:2 * j + 2, :, :], mod[:, SH_M, 2 * j:2 * j + 2])

            for half in range(2):
                base = B_FF + half * (U_FF1 + U_FF2)
                use1 = (USE_FF1A, USE_FF1B)[half]
                with sc.Fori(0, 4) as it:
                    for b in range(2):
                        for j in range(8):
                            hi(base + LAG, 16, it, 8 * b + j)
                        copy_low(use1 + b, base + 8 * b + 8, 16, it)
                        sc.wait_ge(relu2, 8 * half + b + 1 + 2 * it)
                        sc.activation(act[:, bass.ds(4 * b + 8 * it, 4), 0, :], tmp2[:, :, :],
                                      ACT.Copy).then_inc(act_hi, 1)

                def down(it, last=False):
                    for b in range(2):
                        for j in range(16):
                            if not (last and b == 1 and j >= 16 - LAG):
                                hi(base + U_FF1 + LAG, 32, it, 16 * b + j)
                        if last and b == 1:
                            square_tiles(12, 10)
                        elif half == 1:
                            square(8 + b + 1, it, 4 * b + 8 * it, 7 + b + 2 * it)

                if half == 0:
                    with sc.Fori(0, 2) as it:
                        down(it)
                else:
                    down(0)
                    down(1, last=True)
            root(5)

        @block.gpsimd
        def _(gp):
            def lo(u0, step, it, j):
                if (u0 + j) % 2 == 1:
                    slot = (u0 + j) % RING
                    gp.wait_ge(hi_done, u0 + j + 1 + step * it)
                    gp.tensor_tensor(w_lo[:, slot, :, :], raw[:, slot, :, :],
                                     w_hi[:, slot, :, :].bitcast(F32), ALU.subtract).then_inc(lo_pool, 1)

            def add_squares(n):
                gp.wait_ge(sq_done, n)
                gp.tensor_tensor(ssq[:, :, :], ssq[:, :, :], sq[:, :, :], ALU.add).then_inc(ssq_done, 1)

            gp.memset(ssq[:, :, :], 0.0).then_inc(zeroed, 1)
            gp.memset(pT[:, :, :], 0.0).then_inc(part_added, 1)
            gp.wait_ge(zeroed, 1)
            for b in range(4):
                add_squares(b + 1)
            for j in range(RING):
                lo(0, 0, 0, j)
            for q in range(4):
                with gp.Fori(0, 4) as it:
                    for b in range(2):
                        for j in range(2):
                            lo(QC * q + LAG, 4, it, 2 * b + j)
                        gp.wait_ge(psum_free, use_in(q, b) + 2 + 2 * it)
                        gp.wait_ge(part_added, 8 * q + b + 1 + 2 * it)
                        part = pT[:, bass.ds(4 * b + 8 * it, 4), :]
                        gp.tensor_tensor(part, part, tmp2[:, :, :], ALU.add).then_inc(part_added, 1)
            gp.memset(foxA[:, :], 0.0).then_inc(fox_filled, 1)
            gp.memset(foxG[:, :], 0.0).then_inc(fox_filled, 1)
            gp.wait_ge(fox_filled, 2)
            gp.memset(foxA[32:32 + H, :], 1.0).then_inc(fox_filled, 1)
            gp.wait_ge(fox_filled, 3)
            gp.memset(foxG[0:H, :], 1.0).then_inc(fox_filled, 1)
            gp.wait_ge(fox_filled, 4)
            for j in range(LAG, U_LAT + LAG):
                lo(B_LAT, 0, 0, j)

            def stick_weight(i):
                gp.wait_ge(stick_done, i // 3 + 1)
                z = zm[:, i % ZM, :]
                gp.tensor_tensor(z, z, stick[:, i // 3 % 2, :], ALU.subtract).then_inc(log_p_done, 1)

            def fox_operand(i):
                n = i // 3
                if n >= 2:
                    gp.wait_ge(scores_done, i - 5)
                gp.tensor_scalar(foxB[:, n % 2, :], foxG[:, :], consts[:, K_SEL + n:K_SEL + n + 1], None,
                                 ALU.mult).then_inc(fox_b_ready, 1)

            def out_square(i):
                d = width(i)
                gp.wait_ge(out_read, i + 1)
                if i >= 2:
                    gp.wait_ge(out_summed, i - 1)
                for q in range(2):
                    o = o_tok[q][:, head_col(i):head_col(i) + d]
                    ins = gp.tensor_tensor(osq[i % 2][:, q * d:q * d + d], o, o, ALU.mult)
                ins.then_inc(out_squared, 1)

            gp.wait_ge(neg_f_ready, 1)
            for t in range(STEPS):
                if t + 2 < HEADS and kind(t + 2) == FX:
                    fox_operand(t + 2)
                if 0 <= t - STICK < HEADS and kind(t - STICK) == SB:
                    stick_weight(t - STICK)
                if 0 <= t - READ < HEADS:
                    out_square(t - READ)
            gp.wait_ge(inverse_done, 2 * H + 1)
            o = o_tok[1][:, H * VD:].rearrange("p (h d) -> p h d", d=DH)
            gp.tensor_tensor(o, o, hss[:, 0:2 * H, 1].unsqueeze(2).to_broadcast([P, 2 * H, DH]),
                             ALU.mult).then_inc(normed_pool, 1)
            gp.memset(ssq[:, :, :], 0.0).then_inc(zeroed, 1)
            gp.wait_ge(zeroed, 2)
            for b in range(4):
                for j in range(8):
                    lo(B_OUT + LAG, 0, 0, 8 * b + j)
                if b < 3:
                    add_squares(6 + b + 1)
            gp.wait_ge(psum_ready, READY["ffn norm"])
            gp.memset(ssq[:, :, :], 0.0).then_inc(zeroed, 1)
            gp.wait_ge(zeroed, 3)
            for half in range(2):
                base = B_FF + half * (U_FF1 + U_FF2)
                with gp.Fori(0, 4) as it:
                    for j in range(16):
                        lo(base + LAG, 16, it, j)

                def down(it, last=False):
                    for b in range(2):
                        for j in range(16):
                            if not (last and b == 1 and j >= 16 - LAG):
                                lo(base + U_FF1 + LAG, 32, it, 16 * b + j)
                        if half == 1 and not (last and b == 1):
                            add_squares(13 + b + 1 + 2 * it)

                if half == 0:
                    with gp.Fori(0, 2) as it:
                        down(it)
                else:
                    down(0)
                    down(1, last=True)

        @block.vector
        def _(ve):
            def lo(u0, step, it, j):
                if (u0 + j) % 2 == 0:
                    slot = (u0 + j) % RING
                    ve.wait_ge(hi_done, u0 + j + 1 + step * it)
                    ve.tensor_tensor(w_lo[:, slot, :, :], raw[:, slot, :, :],
                                     w_hi[:, slot, :, :].bitcast(F32), ALU.subtract).then_inc(lo_vec, 1)

            def add_chunk(a0, kt0, zeros, step, it, j):
                slot = (a0 + j) % ADA
                early = a0 < A_GA
                half = (a0 // QC) % 2 if early else (a0 + j) % 2
                kt = kt0 + j + step * it if early else kt0 + j // 2 + (step // 2) * it
                ve.wait_ge(ada_full[slot], 16 * ((a0 + j) // ADA + 1) + (16 * step // ADA) * it)
                ve.wait_ge(acc_done, a0 + j - (0 if early else 1) + zeros + step * it)
                dst = accA[:, half * AC:(half + 1) * AC]
                ve.scalar_tensor_tensor(out=dst, in0=ada[:, slot, :], scalar=c_act[:, bass.ds(kt, 1)],
                                        in1=dst, op0=ALU.mult, op1=ALU.add).then_inc(acc_done, 1)

            def clear_acc(halves, chunks, zeros):
                lo_h, hi_h = halves
                ve.memset(accA[:, lo_h * AC:hi_h * AC], 0.0).then_inc(acc_done, 1)
                ve.wait_ge(acc_done, chunks + zeros)

            def mean(use, bank, half, width):
                return ve.tensor_scalar(rstd[:, half, :], ps[use % 2][:, bank, 0:S], 1.0 / width, EPS,
                                        ALU.mult, ALU.add)

            def invert(n, done, halves=1):
                ve.wait_ge(root_done, n)
                ve.reciprocal(rstd[:, 0:halves, :], rstd[:, 0:halves, :]).then_inc(rstd_ready, 1)
                ve.wait_ge(rstd_ready, done)

            def read_mod(use, bank, g, k0=0, n=KT, at=0):
                src = C_B + KT * g + k0
                return ve.tensor_tensor(mod[:, g, k0:k0 + n], ps[use % 2][:, bank, at:at + n],
                                        cols[:, src:src + n], ALU.add)

            def make_gain(g, c, k0=0, n=KT):
                ve.scalar_tensor_tensor(out=gain[:, k0:k0 + n], in0=mod[:, g, k0:k0 + n], scalar=1.0,
                                        in1=cols[:, c + k0:c + k0 + n], op0=ALU.add,
                                        op1=ALU.mult).then_inc(gain_ready, 1)

            def slot_of(n):
                return tmp[:, 2 * (n % 2):2 * (n % 2) + 2, :]

            def scaled_pair(n, src, g, half):
                if n >= 2:
                    ve.wait_ge(op_lo, n - 1)
                for k in range(2):
                    ins = ve.scalar_tensor_tensor(out=slot_of(n)[:, k, :], in0=src[:, k, :], scalar=g[:, k:k + 1],
                                                  in1=rstd[:, half, :], op0=ALU.mult, op1=ALU.mult)
                ins.then_inc(t_ready, 1)

            def operand_lo(n, dst, bias):
                ve.wait_ge(op_hi, n + 1)
                if bias is None:
                    ve.tensor_tensor(dst[:, :, 1, :], slot_of(n), dst[:, :, 0, :].bitcast(F32),
                                     ALU.subtract).then_inc(op_lo, 1)
                else:
                    for k in range(2):
                        ins = ve.scalar_tensor_tensor(out=dst[:, k, 1, :], in0=slot_of(n)[:, k, :],
                                                      scalar=bias[:, k:k + 1], in1=dst[:, k, 0, :].bitcast(F32),
                                                      op0=ALU.add, op1=ALU.subtract)
                    ins.then_inc(op_lo, 1)

            def modulated_norm(r0, shift, j0, j1):
                for j in range(j0, j1 + 1):
                    if j < j1:
                        scaled_pair(r0 + j, xT[:, 2 * j:2 * j + 2, :], gain[:, 2 * j:2 * j + 2], 0)
                    if j > j0:
                        i = j - 1
                        operand_lo(r0 + i, hT[:, 2 * i:2 * i + 2, :, :], mod[:, shift, 2 * i:2 * i + 2])

            def sum_halves(dst, use, n_use, e, n_e, it, done):
                ve.wait_ge(tmp_ready, e + 1 + n_e * it)
                ve.tensor_tensor(dst, ps[use % 2][:, :, 0:S], tmp[:, :, :], ALU.add).then_inc(done, 1)

            def gate_block(use, used, step, blocks, blk, g, it):
                ve.wait_ge(unit_used, used + step * it)
                for half, done in ((1, x_half), (0, x_new)):
                    for n in range(4):
                        if half == 0:
                            ve.wait_ge(x_half, 4 * blocks + n + 1 + 8 * it)
                        x = xT[:, bass.ds(blk + n, 1), :].rearrange("p k t -> p (k t)")
                        ve.scalar_tensor_tensor(out=x, in0=ps[use % 2][:, n, half * S:(half + 1) * S],
                                                scalar=mod[:, g, bass.ds(blk + n, 1)], in1=x,
                                                op0=ALU.mult, op1=ALU.add).then_inc(done, 1)
                ve.wait_ge(x_new, 4 * blocks + 4 + 8 * it)
                ve.sem_inc(psum_free, 1)

            ve.sem_inc(psum_free, 1)
            clear_acc((0, 1), 0, 1)
            ve.wait_ge(silu_step, 1)
            den = small[:, 0:KT]
            ve.tensor_scalar(den, c_act[:, :], 1.0, None, ALU.add).then_inc(silu_step, 1)
            ve.wait_ge(silu_step, 2)
            ve.reciprocal(den, den).then_inc(silu_step, 1)
            ve.wait_ge(silu_step, 3)
            ve.tensor_tensor(c_act[:, :], cols[:, C_C:C_C + KT], den, ALU.mult).then_inc(silu_step, 1)
            ve.wait_ge(silu_step, 4)
            with ve.Fori(0, QC // 4) as it:
                for j in range(4):
                    add_chunk(0, 0, Z_Q(0), 4, it, j)
            for j in range(RING):
                lo(0, 0, 0, j)
            for q in range(4):
                use = 9 * q
                ve.wait_ge(psum_ready, READY[use])
                if q == 0:
                    mean(use, 1, 0, D).then_inc(mean_done, 1)
                read_mod(use, 0, SC_A, QT * q, QT, 0).then_inc(mod_ready, 1)
                read_mod(use, 0, SH_A, QT * q, QT, QT).then_inc(mod_ready, 1)
                ve.wait_ge(mod_ready, 2 * q + 2)
                if q == 0:
                    ve.wait_ge(mean_done, 1)
                ve.sem_inc(psum_free, 1)
                make_gain(SC_A, C_MIX, QT * q, QT)
                ve.wait_ge(gain_ready, q + 1)
                if q == 0:
                    invert(1, 1)
                modulated_norm(R_MIX, SH_A, 2 * q, 2 * q + 2)
                halves = ((q + 1) % 2, (q + 1) % 2 + 1) if q < 3 else (0, 2)
                clear_acc(halves, QC * (q + 1), Z_Q(q + 1))
                with ve.Fori(0, 4) as it:
                    for b in range(2):
                        for j in range(2 * b, 2 * b + 2):
                            lo(QC * q + LAG, 4, it, j)
                            add_chunk(QC * (q + 1), 0, Z_Q(q + 1), 4, it, j)
                        ve.wait_ge(part_added, 8 * q + b + 1 + 2 * it)
                        sum_halves(tmp2[:, :, :], use_in(q, b), 2, 8 * q + b, 2, it, psum_free)
            ve.wait_ge(psum_ready, READY[USE_LSTAT])
            ve.wait_ge(part_added, 33)
            mean(USE_LSTAT, 0, 0, QL)
            mean(USE_LSTAT, 1, 1, KVL).then_inc(mean_done, 1)
            ve.wait_ge(mean_done, 2)
            ve.sem_inc(psum_free, 1)
            invert(2, 2, halves=2)
            for n in range(4):
                if n < 3:
                    g = C_QN + 2 * n
                    scaled_pair(R_CQ + n, pT[:, T_CQ + 2 * n:T_CQ + 2 * n + 2, :], cols[:, g:g + 2], n // 2)
                if n:
                    operand_lo(R_CQ + n - 1, lat[:, 2 * n - 2:2 * n, :, :], None)
            fx, fl = foxB[0:H, 0, :], foxB[0:H, 1, :]
            ve.tensor_scalar(fx, pT[0:H, T_F, :], cols[0:H, C_BF:C_BF + 1], None, ALU.add).then_inc(forget_step, 1)
            ve.tensor_scalar(pT[:, T_SB:T_SB + 4, :], pT[:, T_SB:T_SB + 4, :], DH ** -0.5, None,
                             ALU.mult).then_inc(q_scaled, 1)
            ve.tensor_scalar(pT[:, T_FX:T_FX + 4, :], pT[:, T_FX:T_FX + 4, :], DH ** -0.5, None,
                             ALU.mult).then_inc(q_scaled, 1)
            ve.wait_ge(forget_step, 4)
            ve.scalar_tensor_tensor(out=fx, in0=fx, scalar=0.0, in1=fl, op0=ALU.min,
                                    op1=ALU.subtract).then_inc(forget_step, 1)
            ve.wait_ge(forget_step, 5)
            ve.wait_ge(fox_filled, 2)
            ve.tensor_tensor_scan(foxA[0:H, :], consts[0:H, K_SEG:K_SEG + 1].to_broadcast([H, S]), fx, 0.0,
                                  ALU.mult, ALU.add).then_inc(forget_step, 1)
            dests = [q_nope[:, 0:4, :], q_nope[:, 4:8, :], rope_raw[:, :, :], k_nope[:, 0:4, :],
                     k_nope[:, 4:8, :], vT[:, 0:4, :], vT[:, 4:8, :]]
            for n, e in enumerate(LAT_ENDS):
                for u in range(LAG if n == 0 else LAT_ENDS[n - 1] + 1 + LAG, e + 1 + LAG):
                    lo(B_LAT, 0, 0, u)
                for j in range(QC + 2 * n, QC + 2 * n + 2):
                    add_chunk(A_GA, 0, Z_GA, 0, 0, j)
                sum_halves(dests[n], USE_LAT + n, 0, E_LAT + n, 0, 0, psum_free)
            for j in range(QC + 14, CPS):
                add_chunk(A_GA, 0, Z_GA, 0, 0, j)
            cos, sin = consts[:, K_COS:K_COS + S], consts[:, K_SIN:K_SIN + S]
            cos4 = cos.unsqueeze(1).to_broadcast([P, 4, S])
            sin4 = sin.unsqueeze(1).to_broadcast([P, 4, S])
            rot = ps[USE_ROT % 2]
            ve.tensor_tensor(q_rope[:, :, :], rope_raw[:, :, :], cos4, ALU.mult).then_inc(rope_term, 1)
            ve.tensor_tensor(rstd[:, 0, :], pT[:, T_KR, :], cos, ALU.mult).then_inc(rope_term, 1)
            ve.wait_ge(psum_ready, READY[USE_ROT])
            ve.tensor_tensor(tmp2[:, :, :], rot[:, 0:2, :].rearrange("p b (h t) -> p (b h) t", h=2), sin4,
                             ALU.mult).then_inc(rope_term, 1)
            ve.tensor_tensor(rstd[:, 1, :], rot[:, 2, 0:S], sin, ALU.mult).then_inc(rope_term, 1)
            ve.wait_ge(rope_term, 4)
            ve.sem_inc(psum_free, 1)
            ve.tensor_tensor(q_rope[:, :, :], q_rope[:, :, :], tmp2[:, :, :], ALU.add).then_inc(rope_done, 1)
            ve.tensor_tensor(pT[:, T_KR, :], rstd[:, 0, :], rstd[:, 1, :], ALU.add).then_inc(rope_done, 1)
            ve.wait_ge(v_copied, 1)
            ve.tensor_copy(v_mla[:, 1, :], ps[USE_VM % 2][:, 2:4, :].rearrange("p a b -> p (a b)"))\
                .then_inc(psum_free, 1)
            ve.wait_ge(v_copied, 2)
            ve.tensor_copy(v_fx, ps[USE_VS % 2][:, 2:4, :]).then_inc(psum_free, 1)
            ve.wait_ge(psum_ready, READY[USE_GA])
            read_mod(USE_GA, 0, G_A).then_inc(mod_ready, 1)
            ve.wait_ge(mod_ready, 9)
            ve.sem_inc(psum_free, 1)
            clear_acc((0, 2), A_SHM, Z_SHM)

            def masked_scores(i):
                s = ps[0][:, i % 2, 0:3 * P]
                z = zm[:, i % ZM, :]
                ve.wait_ge(scores_done, i + 1)
                if i >= ZM:
                    ve.wait_ge(probs_ready, i - ZM + 1)
                if kind(i) == ML:
                    ve.scalar_tensor_tensor(out=z, in0=s, scalar=(NOPE + ROPE) ** -0.5,
                                            in1=consts[:, K_MLA:K_MLA + 3 * P], op0=ALU.mult,
                                            op1=ALU.add).then_inc(masked, 1)
                else:
                    k = K_SB if kind(i) == SB else K_FOX
                    ve.tensor_tensor(z, s, consts[:, k:k + 3 * P], ALU.add).then_inc(masked, 1)
                if kind(i) != SB:
                    ve.wait_ge(masked, i + 1)
                    ve.tensor_reduce(mx[:, place(i), 0:1], z[:, 0:P], AX.X, ALU.max, negate=True).then_inc(max_done, 1)
                    ve.tensor_reduce(mx[:, place(i), 1:2], z[:, P:3 * P], AX.X, ALU.max, negate=True).then_inc(max_done, 1)

            def stick_sums(i):
                n = i // 3
                e, z, r = el[:, n % 2, :], zm[:, i % ZM, :], stick[:, n % 2, :]
                ve.wait_ge(ln_done, n + 1)
                ve.scalar_tensor_tensor(out=e, in0=z, scalar=0.0, in1=e, op0=ALU.max,
                                        op1=ALU.add).then_inc(softplus_done, 1)
                ve.wait_ge(softplus_done, n + 1)
                if n >= 2:
                    ve.wait_ge(log_p_done, n - 1)
                ve.tensor_tensor_scan(r[:, ::-1], consts[:, K_SEG:K_SEG + 3 * P][:, ::-1], e[:, ::-1], 0.0,
                                      ALU.mult, ALU.add).then_inc(stick_done, 1)

            def read_output(i):
                d, c, at = width(i), head_col(i), place(i)
                ve.wait_ge(out_ready, i + 1)
                if kind(i) != SB:
                    ve.reciprocal(rinv[:, at, :], row[:, at, :]).then_inc(inverse_done, 1)
                    ve.wait_ge(inverse_done, softmaxes(i) + 1)
                for q in range(2):
                    o, src = o_tok[q][:, c:c + d], ps[1][:, i % 2, q * d:(q + 1) * d]
                    if kind(i) != SB:
                        ins = ve.tensor_scalar(o, src, rinv[:, at, q:q + 1], None, ALU.mult)
                    else:
                        ins = ve.tensor_copy(o, src)
                ins.then_inc(out_read, 1)

            def sum_squares(i):
                d = width(i)
                ve.wait_ge(out_squared, i + 1)
                ve.tensor_reduce(hss[:, place(i), :], osq[i % 2][:, 0:2 * d].rearrange("p (q d) -> p q d", q=2),
                                 AX.X, ALU.add).then_inc(out_summed, 1)

            for t in range(STEPS + 1):
                if 0 <= t - MASK < HEADS:
                    masked_scores(t - MASK)
                if 0 <= t - STICK < HEADS and kind(t - STICK) == SB:
                    stick_sums(t - STICK)
                if 0 <= t - READ < HEADS:
                    read_output(t - READ)
                if 0 <= t - SUM < HEADS:
                    sum_squares(t - SUM)
                for j in range(min(CPS, CPS * t // (STEPS - 4)), min(CPS, CPS * (t + 1) // (STEPS - 4))):
                    add_chunk(A_SHM, 0, Z_SHM, 0, 0, j)
            ve.wait_ge(out_summed, HEADS)
            narrow = hss[:, 0:2 * H, :]
            ve.tensor_scalar(narrow, narrow, 1.0 / DH, EPS, ALU.mult, ALU.add)
            ve.tensor_scalar(hss[:, 2 * H:HEADS, :], hss[:, 2 * H:HEADS, :], 1.0 / VD, EPS, ALU.mult,
                             ALU.add).then_inc(mean_done, 1)
            ve.wait_ge(root_done, 3)
            ve.reciprocal(hss[:, :, :], hss[:, :, :]).then_inc(inverse_done, 1)
            ve.wait_ge(inverse_done, 2 * H + 1)
            for first, n, d, c, tiles in ((2 * H, H, VD, 0, (0, 1)), (0, 2 * H, DH, H * VD, (0,))):
                for q in tiles:
                    o = o_tok[q][:, c:c + n * d].rearrange("p (h d) -> p h d", d=d)
                    ve.tensor_tensor(o, o, hss[:, first:first + n, q].unsqueeze(2).to_broadcast([P, n, d]),
                                     ALU.mult).then_inc(normed_vec, 1)
            for j in range(8):
                use = USE_OT + j // 4
                ve.wait_ge(op_hi, R_O + j + 1)
                for k in range(2):
                    c = C_OUT + 2 * j + k
                    ins = ve.scalar_tensor_tensor(
                        out=hT[:, 2 * j + k, 1, :], in0=ps[use % 2][:, j % 4, k * S:(k + 1) * S],
                        scalar=cols[:, c:c + 1], in1=hT[:, 2 * j + k, 0, :].bitcast(F32),
                        op0=ALU.mult, op1=ALU.subtract)
                ins.then_inc(op_lo, 1)
                if j % 4 == 3:
                    ve.wait_ge(op_lo, R_O + j + 1)
                    ve.sem_inc(psum_free, 1)

            ve.wait_ge(psum_ready, READY[USE_SHM])
            read_mod(USE_SHM, 0, SH_M).then_inc(mod_ready, 1)
            ve.wait_ge(mod_ready, 10)
            ve.sem_inc(psum_free, 1)
            clear_acc((0, 2), A_SCM, Z_SCM)
            for j in range(ADA):
                add_chunk(A_SCM, 0, Z_SCM, 0, 0, j)
            for b in range(4):
                for j in range(8 * b, 8 * b + 8):
                    lo(B_OUT + LAG, 0, 0, j)
                    if ADA + j < CPS:
                        add_chunk(A_SCM, 0, Z_SCM, 0, 0, ADA + j)
                gate_block(USE_OUT + b, B_OUT + 8 * b + 8, 0, b, 4 * b, G_A, 0)
            ve.wait_ge(psum_ready, READY[USE_FFN])
            read_mod(USE_FFN, 0, SC_M).then_inc(mod_ready, 1)
            ve.wait_ge(mod_ready, 11)
            make_gain(SC_M, C_FFN)
            ve.wait_ge(gain_ready, 5)
            ve.wait_ge(psum_ready, READY["ffn norm"])
            mean(USE_FFN, 1, 0, D).then_inc(mean_done, 1)
            ve.wait_ge(mean_done, 4)
            ve.sem_inc(psum_free, 1)
            invert(4, 3)
            modulated_norm(R_FFN, SH_M, 0, 8)
            clear_acc((0, 2), A_GM, Z_GM)

            for half in range(2):
                base = B_FF + half * (U_FF1 + U_FF2)
                use1, e1 = ((USE_FF1A, E_FF1A), (USE_FF1B, E_FF1B))[half]
                with ve.Fori(0, 4) as it:
                    for b in range(2):
                        for j in range(8 * b, 8 * b + 8):
                            lo(base + LAG, 16, it, j)
                            if half == 0 and j % 2 == 1:
                                add_chunk(A_GM, 0, Z_GM, 8, it, 4 * b + j % 8 // 2)
                        sum_halves(tmp2[:, :, :], use1 + b, 2, e1 + b, 2, it, psum_free)
                        ve.wait_ge(psum_free, use1 + b + 2 + 2 * it)
                        ve.scalar_tensor_tensor(out=tmp2[:, :, :], in0=tmp2[:, :, :], scalar=0.0,
                                                in1=tmp2[:, :, :], op0=ALU.max, op1=ALU.mult).then_inc(relu2, 1)
                        blk = bass.ds(4 * b + 8 * it, 4)
                        ve.wait_ge(act_hi, 8 * half + b + 1 + 2 * it)
                        ve.tensor_tensor(act[:, blk, 1, :], tmp2[:, :, :], act[:, blk, 0, :].bitcast(F32),
                                         ALU.subtract).then_inc(act_lo, 1)
                use2 = (USE_FF2A, USE_FF2B)[half]
                if half == 0:
                    ve.wait_ge(psum_ready, READY[USE_GM])
                    read_mod(USE_GM, 0, G_M).then_inc(mod_ready, 1)
                    ve.wait_ge(mod_ready, 12)
                    ve.sem_inc(psum_free, 1)

                def down(it, last=False):
                    for b in range(2):
                        for j in range(16):
                            if not (last and b == 1 and j >= 16 - LAG):
                                lo(base + U_FF1 + LAG, 32, it, 16 * b + j)
                        gate_block(use2 + b, base + U_FF1 + 16 * b + 16, 32, 4 + 4 * half + b,
                                   4 * b + 8 * it, G_M, it)

                if half == 0:
                    with ve.Fori(0, 2) as it:
                        down(it)
                else:
                    down(0)
                    down(1, last=True)
            ve.wait_ge(psum_ready, READY[USE_END])
            mean(USE_END, 0, 0, D).then_inc(mean_done, 1)
            invert(5, 4)
            for k in range(KT):
                dst = (tmp, tmp2, sq, ssq)[k // 4]
                ve.scalar_tensor_tensor(out=dst[:, k % 4, :], in0=xT[:, k, :], scalar=cols[:, C_FIN + k:C_FIN + k + 1],
                                        in1=rstd[:, 0, :], op0=ALU.mult, op1=ALU.mult).then_inc(result_ready, 1)

        @block.tensor
        def _(pe):
            def take(use, n_use=0, it=0):
                if use >= 1:
                    pe.wait_ge(psum_free, use + n_use * it)

            def unit(u0, step, it, j, out_set, rhs, kt0, ready, first, last):
                slot = (u0 + j) % RING
                pe.wait_ge(*ready)
                pe.wait_ge(hi_done, u0 + j + 1 + step * it)
                for k in range(UK):
                    for n in range(4):
                        pe.matmul(out_set[:, n, :], w_hi[:, slot, k, n * P:(n + 1) * P], rhs[:, kt0 + k, :, :],
                                  start=first and k == 0, stop=False)
                pe.wait_ge(lo_sem(u0 + j), lo_count(u0, step, it, j))
                for k in range(UK):
                    for n in range(4):
                        ins = pe.matmul(out_set[:, n, 0:S], w_lo[:, slot, k, n * P:(n + 1) * P],
                                        rhs[:, kt0 + k, 0, :], start=False, stop=last and k == UK - 1)
                ins.then_inc(unit_used, 1)

            def product(u0, step, it, j0, units, use, n_use, rhs, kt0, ready):
                take(use, n_use, it)
                for j in range(units):
                    unit(u0, step, it, j0 + j, ps[use % 2], rhs, kt0 + UK * j, ready(j), j == 0, j == units - 1)

            def column_sums(use, k0=0, n=KT):
                for k in range(n):
                    ins = pe.matmul(ps[use % 2][:, 0, k:k + 1], accA[:, (k0 + k) * P:(k0 + k + 1) * P],
                                    ones[:, 0:1], start=True, stop=True)
                ins.then_inc(psum_ready, 1)

            def token_sums(use, bank, src, n):
                for k in range(n):
                    ins = pe.matmul(ps[use % 2][:, bank, 0:S], ones, src[:, k, :], start=(k == 0), stop=(k == n - 1))
                return ins

            def residual_sums(use, bank, added, squares):
                s = ps[use % 2][:, bank, 0:S]
                pe.wait_ge(ssq_done, added)
                for k in range(4):
                    pe.matmul(s, ones, ssq[:, k, :], start=(k == 0), stop=False)
                for k in range(4):
                    pe.wait_ge(sq_done, squares + k + 1)
                    ins = pe.matmul(s, ones, sq[:, k, :], start=False, stop=(k == 3))
                ins.then_inc(psum_ready, 1)

            pe.wait_ge(ld_cols, 16)
            pe.wait_ge(ssq_done, 4)
            token_sums(0, 1, ssq, 4)
            for q in range(4):
                take(9 * q)
                pe.wait_ge(acc_done, QC * (q + 1) + Z_Q(q))
                column_sums(9 * q, q % 2 * 8, 8)
                with pe.Fori(0, 4) as it:
                    for b in range(2):
                        product(QC * q, 4, it, 2 * b, 2, use_in(q, b), 2, hT, QT * q,
                                lambda j: (op_lo, R_MIX + 2 * q + j + 1))
            take(USE_LSTAT)
            pe.wait_ge(sq_done, 5)
            token_sums(USE_LSTAT, 0, tmp2, 4).then_inc(cq_summed, 1)
            pe.wait_ge(sq_done, 6)
            token_sums(USE_LSTAT, 1, tmp2, 2).then_inc(psum_ready, 1)
            for n in range(3):
                product(B_LAT, 0, 0, 2 * n, 2, USE_LAT + n, 0, lat, 0, lambda j: (op_lo, R_CQ + j + 1))
            for n in range(4):
                product(B_LAT, 0, 0, U_UQ + n, 1, USE_LAT + 3 + n, 0, lat, 4, lambda j: (op_lo, R_CKV + 1))
            pe.wait_ge(ld_const, 16)
            take(USE_ROT)
            rotate = consts[:, K_ROT:K_ROT + P]
            for b in range(2):
                pe.matmul(ps[USE_ROT % 2][:, b, :], rotate, rope_raw[:, 2 * b:2 * b + 2, :], start=True, stop=True)
            pe.matmul(ps[USE_ROT % 2][:, 2, 0:S], rotate, pT[:, T_KR, :], start=True, stop=True)\
                .then_inc(psum_ready, 1)
            pe.wait_ge(psum_free, USE_LAT + 8)
            for t in range(2):
                for k in range(H):
                    ins = pe.transpose(ps[USE_VM % 2][:, 2 * t + k // 4, (k % 4) * P:(k % 4 + 1) * P],
                                       vT[:, k, t * P:(t + 1) * P], ident)
            ins.then_inc(psum_ready, 1)
            take(USE_VS)
            for g, t0 in ((0, T_SB + 8), (1, T_FX + 8)):
                for t in range(2):
                    for k in range(4):
                        ins = pe.transpose(ps[USE_VS % 2][:, 2 * g + t, k * P:(k + 1) * P],
                                           pT[:, t0 + k, t * P:(t + 1) * P], ident)
            ins.then_inc(psum_ready, 1)

            take(USE_GA)
            pe.wait_ge(acc_done, A_SHM + Z_GA)
            column_sums(USE_GA)

            def scores(i):
                s = ps[0][:, i % 2, :]
                n, tile, r = i // 3, i // 3 // 2, DH * (i // 3 % 2)
                if kind(i) != ML:
                    t0 = (T_SB if kind(i) == SB else T_FX) + tile
                    terms = [(pT[r:r + DH, t0, :], pT[r:r + DH, t0 + 4, :])]
                    if kind(i) == FX:
                        terms.append((foxA[:, :], foxB[:, n % 2, :]))
                else:
                    terms = [(q_nope[:, n, :], k_nope[:, n, :]),
                             (q_rope[r:r + DH, tile, :], pT[r:r + DH, T_KR, :])]
                if i >= 2:
                    pe.wait_ge(masked, i - 1)
                if kind(i) == FX:
                    pe.wait_ge(fox_b_ready, n + 1)
                for q in range(2):
                    for m, (lhs, rhs) in enumerate(terms):
                        ins = pe.matmul(s[:, q * P:(2 * q + 1) * P],
                                        lhs[:, q * P:(q + 1) * P], rhs[:, 0:(q + 1) * P],
                                        start=(m == 0), stop=(m == len(terms) - 1))
                ins.then_inc(scores_done, 1)

            def transpose_p(i):
                pe.wait_ge(probs_ready, i + 1)
                if i >= 2:
                    pe.wait_ge(probs_copied, i - 1)
                for b in range(3):
                    ins = pe.transpose(ps[0][:, 2 + i % 2, b * P:(b + 1) * P], probs[i % 2][:, b * P:(b + 1) * P],
                                       ident)
                ins.then_inc(probs_turned, 1)

            def weigh_v(i):
                d, n = width(i), i // 3
                v = (v_sb, v_mla, v_fx)[kind(i)][:, :, n * d:(n + 1) * d]
                pe.wait_ge(probs_copied, i + 1)
                if i >= 2:
                    pe.wait_ge(out_read, i - 1)
                o, pt = ps[1][:, i % 2, :], probsT[i % 2]
                pe.matmul(o[:, 0:d], pt[:, 0:P], v[:, 0, :], start=True, stop=True)
                pe.matmul(o[:, d:2 * d], pt[:, P:2 * P], v[:, 0, :], start=True, stop=False)
                pe.matmul(o[:, d:2 * d], pt[:, 2 * P:3 * P], v[:, 1, :], start=False, stop=True).then_inc(out_ready, 1)

            pe.wait_ge(psum_free, USE_GA + 2)
            pe.wait_ge(q_scaled, 2)
            pe.wait_ge(rope_done, 2)
            pe.wait_ge(neg_f_ready, 1)
            pe.wait_ge(fox_filled, 4)
            for t in range(STEPS):
                if t < HEADS:
                    scores(t)
                if 0 <= t - TURN < HEADS:
                    transpose_p(t - TURN)
                if 0 <= t - MIX < HEADS:
                    weigh_v(t - MIX)
            for k in range(KT):
                use = USE_OT + k // 8
                pe.wait_ge(normed_vec, 2 + k // 8)
                if k >= 8:
                    pe.wait_ge(normed_pool, 1)
                for q in range(2):
                    c = (k % 2) * S + q * P
                    ins = pe.transpose(ps[use % 2][:, k % 8 // 2, c:c + P], o_tok[q][:, k * P:(k + 1) * P], ident)
                if k % 8 == 7:
                    ins.then_inc(psum_ready, 1)
            take(USE_SHM)
            pe.wait_ge(acc_done, A_SCM + Z_SHM)
            column_sums(USE_SHM)
            for b in range(4):
                product(B_OUT, 0, 0, 8 * b, 8, USE_OUT + b, 0, hT, 0, lambda j: (op_lo, R_O + j + 1))
            take(USE_FFN)
            pe.wait_ge(acc_done, A_GM + Z_SCM)
            column_sums(USE_FFN)
            residual_sums(USE_FFN, 1, 7, 9)
            for half in range(2):
                base = B_FF + half * (U_FF1 + U_FF2)
                use1, use2 = ((USE_FF1A, USE_FF2A), (USE_FF1B, USE_FF2B))[half]
                with pe.Fori(0, 4) as it:
                    for b in range(2):
                        product(base, 16, it, 8 * b, 8, use1 + b, 2, hT, 0, lambda j: (op_lo, R_FFN + j + 1))
                if half == 0:
                    take(USE_GM)
                    pe.wait_ge(acc_done, A_GM + CPS + Z_GM)
                    column_sums(USE_GM)
                with pe.Fori(0, 2) as it:
                    for b in range(2):
                        product(base + U_FF1, 32, it, 16 * b, 16, use2 + b, 2, act, 0,
                                lambda j: (act_lo, 8 * half + j // 2 + 1))
            take(USE_END)
            residual_sums(USE_END, 0, 10, 16)


def feature_columns(v):
    return np.asarray(v).reshape(-1, P).T


def shape_constants():
    c = np.zeros((P, K_END), np.float32)
    c[:, K_ID:K_ID + P] = np.eye(P, dtype=np.float32)
    m = np.arange(P)
    low = m % ROPE < ROPE // 2
    c[m[low] + ROPE // 2, K_ROT + m[low]] = -1.0
    c[m[~low] - ROPE // 2, K_ROT + m[~low]] = 1.0
    inv = np.float32(ROPE_BASE) ** (-np.arange(0, ROPE, 2, dtype=np.float32) / np.float32(ROPE))
    ang = np.arange(S, dtype=np.float32)[None, :] * inv[m % (ROPE // 2)][:, None]
    c[:, K_COS:K_COS + S] = np.cos(ang)
    c[:, K_SIN:K_SIN + S] = np.sin(ang)
    q, k = m[:, None], m[None, :]
    for at, allowed in ((K_FOX, k <= q), (K_SB, k < q), (K_MLA, k < (q // CHUNK + 1) * CHUNK)):
        diagonal = np.where(allowed, 0.0, MASKED)
        c[:, at:at + P] = diagonal
        c[:, at + 2 * P:at + 3 * P] = diagonal
    c[:, K_SEG:K_SEG + 3 * P] = 1.0
    c[:, [K_SEG + P - 1, K_SEG + 3 * P - 1]] = 0.0
    for n in range(H):
        c[[n, 32 + n], K_SEL + n] = 1.0
    return c


def units_of(w):
    k, n = w.shape
    return w.reshape(k // (UK * P), UK, P, n // BW, BW).transpose(3, 0, 2, 1, 4).reshape(-1, P, UC)


def kernel(x, c, w_ada, b_ada, norm_mix, w_in, q_norm, w_uq, kv_norm, w_ukv, b_forget,
           out_norm, w_out, norm_ffn, w_ff1, w_ff2, final_norm):
    import concourse.bacc as bacc
    from concourse.bass_utils import run_bass_kernel_spmd

    f32 = np.float32
    a = lambda v: np.asarray(v)
    w_in, w_uq, w_ukv, w_ff1, w_ff2 = (a(w)[0] for w in (w_in, w_uq, w_ukv, w_ff1, w_ff2))
    lat = QL + KVL
    rope, gates = w_in[:, lat:lat + ROPE], w_in[:, -H:]
    pad = np.zeros((D, P - H), f32)
    w_in = np.concatenate([w_in[:, :lat], rope, rope, gates, pad, w_in[:, lat + ROPE:-H]], axis=1)
    uq = w_uq.reshape(QL, H, NOPE + ROPE)
    ukv = w_ukv.reshape(KVL, H, NOPE + VD)
    parts = [w_in[q * QT * P:(q + 1) * QT * P] for q in range(4)]
    parts += [
        uq[:, :, :NOPE].reshape(QL, -1), uq[:, :, NOPE:].reshape(QL, -1),
        ukv[:, :, :NOPE].reshape(KVL, -1), ukv[:, :, NOPE:].reshape(KVL, -1), a(w_out)[0]]
    for h in range(2):
        parts += [w_ff1[:, h * FF // 2:(h + 1) * FF // 2], w_ff2[h * FF // 2:(h + 1) * FF // 2]]
    weights = np.concatenate([units_of(w) for w in parts])
    ada = a(w_ada)[0].reshape(KT, P, 6, D)
    first = [np.concatenate([ada[:, :, g, q * QT * P:(q + 1) * QT * P] for g in (SC_A, SH_A)], axis=-1)
             for q in range(4)]
    later = [ada[:, :, g].reshape(KT, P, D // AC, AC).transpose(0, 2, 1, 3).reshape(-1, P, AC)
             for g in (G_A, SH_M, SC_M, G_M)]
    ada = np.concatenate(first + later)
    cols = np.zeros((P, C_END), f32)
    for at, v in ((C_C, c), (C_B, a(b_ada)[0]), (C_MIX, a(norm_mix)[0]), (C_FFN, a(norm_ffn)[0]),
                  (C_OUT, a(out_norm)[0]), (C_FIN, final_norm), (C_QN, a(q_norm)[0]), (C_KVN, a(kv_norm)[0])):
        v = feature_columns(v)
        cols[:, at:at + v.shape[1]] = v
    cols[:H, C_BF] = a(b_forget)[0]
    cols[:, C_ONE:] = 1.0
    xt = a(x)[0].reshape(S, KT, P).transpose(2, 1, 0).reshape(P, -1)
    arrays = {"xt": xt, "cols": cols, "consts": shape_constants(), "ada": ada, "weights": weights}
    arrays = {n: np.ascontiguousarray(v) for n, v in arrays.items()}

    nc = bacc.Bacc("TRN2", target_bir_lowering=False, num_devices=1)
    aps = [nc.dram_tensor(f"in_{n}", v.shape, F32, kind="ExternalInput").ap() for n, v in arrays.items()]
    y = nc.dram_tensor("y", (P, KT * S), F32, kind="ExternalOutput").ap()
    hybrid_block(nc, *aps, y)
    r = run_bass_kernel_spmd(nc, [{f"in_{n}": v for n, v in arrays.items()}], core_ids=[0])
    got = r.results[0]["y"]
    return np.ascontiguousarray(got.reshape(P, KT, S).transpose(2, 1, 0).reshape(1, S, D))
```
